# Optimizing a Trainium2 kernel written in Bass

```python
import jax
import jax.numpy as jnp
from jax import lax
import numpy as np

D_MODEL = 1024
BATCH = 1
SEQ = 1024
DEPTH = 1

ATT_HEADS = 8
ATT_KV_HEADS = 2
ATT_GROUP = ATT_HEADS // ATT_KV_HEADS
ATT_HEAD_DIM = 64
WINDOW = 128
ATT_BLOCK = 128
ROPE_THETA = 500000.0
ROPE_DIM = ATT_HEAD_DIM // 4

DN_HEADS = 4
DN_KEY_DIM = 128
DN_VAL_DIM = 128
DN_CONV = 4
DN_CHUNK = 64

ATT_Q_W = ATT_HEADS * ATT_HEAD_DIM
ATT_KV_W = ATT_KV_HEADS * ATT_HEAD_DIM
DN_QK_W = DN_HEADS * DN_KEY_DIM
DN_V_W = DN_HEADS * DN_VAL_DIM
DN_QKV_W = 2 * DN_QK_W + DN_V_W
MIX_W = ATT_Q_W + DN_V_W
IN_W = ATT_Q_W + 2 * ATT_KV_W + DN_QKV_W + DN_V_W + 2 * DN_HEADS
IN_SPLITS = (ATT_Q_W,
             ATT_Q_W + ATT_KV_W,
             ATT_Q_W + 2 * ATT_KV_W,
             ATT_Q_W + 2 * ATT_KV_W + DN_QKV_W,
             ATT_Q_W + 2 * ATT_KV_W + DN_QKV_W + DN_V_W,
             ATT_Q_W + 2 * ATT_KV_W + DN_QKV_W + DN_V_W + DN_HEADS)

PEER_HEADS = 8
PEER_KEYS = 128
PEER_EXPERTS = PEER_KEYS * PEER_KEYS
PEER_QDIM = 256
PEER_HALF = PEER_QDIM // 2
PEER_TOPK = 16
PEER_TOKEN_BLOCK = 128

EPS = 1e-6

kernel_name = "hybrid_swa_sink_gdn_peer"

def rms_norm(x, w):
    xf = x.astype(jnp.float32)
    y = xf * lax.rsqrt(jnp.mean(xf * xf, axis=-1, keepdims=True) + EPS)
    return (y * w.astype(jnp.float32)).astype(x.dtype)

def l2_norm(x):
    return x * lax.rsqrt(jnp.sum(x * x, axis=-1, keepdims=True) + EPS)

def partial_rope(x, pos):
    half = ROPE_DIM // 2
    inv_freq = ROPE_THETA ** (-(jnp.arange(half, dtype=jnp.float32) * 2.0 / ROPE_DIM))
    ang = pos.astype(jnp.float32)[:, None] * inv_freq[None, :]
    cos = jnp.cos(ang)[None, :, None, :]
    sin = jnp.sin(ang)[None, :, None, :]
    xr = x[..., :ROPE_DIM].astype(jnp.float32)
    x1, x2 = xr[..., :half], xr[..., half:]
    rot = jnp.concatenate([x1 * cos - x2 * sin, x2 * cos + x1 * sin], axis=-1)
    return jnp.concatenate([rot.astype(x.dtype), x[..., ROPE_DIM:]], axis=-1)

def sliding_window_sink_attention(q, k, v, sinks):
    B, T = q.shape[0], q.shape[1]
    nb = T // ATT_BLOCK
    qb = q.reshape(B, nb, ATT_BLOCK, ATT_KV_HEADS, ATT_GROUP, ATT_HEAD_DIM)

    def band(t):
        tb = t.reshape(B, nb, ATT_BLOCK, ATT_KV_HEADS, ATT_HEAD_DIM)
        prev = jnp.pad(tb, ((0, 0), (1, 0), (0, 0), (0, 0), (0, 0)))[:, :-1]
        return jnp.concatenate([prev, tb], axis=2)

    kb, vb = band(k), band(v)
    s = jnp.einsum('bnqhgd,bnkhd->bnhgqk', qb, kb,
                   preferred_element_type=jnp.float32) * (ATT_HEAD_DIM ** -0.5)
    qi = jnp.arange(ATT_BLOCK)[:, None]
    ki = jnp.arange(2 * ATT_BLOCK)[None, :]
    rel = qi + ATT_BLOCK - ki
    kpos = (jnp.arange(nb)[:, None, None] - 1) * ATT_BLOCK + ki[None]
    valid = (rel >= 0)[None] & (rel < WINDOW)[None] & (kpos >= 0)
    s = jnp.where(valid[None, :, None, None], s, -jnp.inf)
    sink = sinks.astype(jnp.float32).reshape(1, 1, ATT_KV_HEADS, ATT_GROUP, 1, 1)
    m = jnp.maximum(jnp.max(s, axis=-1, keepdims=True), sink)
    p = jnp.exp(s - m)
    probs = p / (jnp.sum(p, axis=-1, keepdims=True) + jnp.exp(sink - m))
    o = jnp.einsum('bnhgqk,bnkhd->bnqhgd', probs.astype(v.dtype), vb)
    return o.reshape(B, T, ATT_HEADS * ATT_HEAD_DIM)

def causal_silu_conv(x, w):
    C = x.shape[-1]
    y = lax.conv_general_dilated(x, w[:, None, :].astype(x.dtype), window_strides=(1,),
                                 padding=((DN_CONV - 1, 0),),
                                 dimension_numbers=('NWC', 'WIO', 'NWC'),
                                 feature_group_count=C)
    return jax.nn.silu(y)

def chunk_gated_delta_rule(q, k, v, g, beta):
    B, T, H, Dk = q.shape
    Dv = v.shape[-1]
    C = DN_CHUNK
    n = T // C
    f32 = jnp.float32
    q = l2_norm(q.astype(f32)) * (Dk ** -0.5)
    k = l2_norm(k.astype(f32))
    v = v.astype(f32)

    def to_chunks(t):
        return jnp.swapaxes(t.reshape((B, n, C) + t.shape[2:]), 2, 3)

    q, k, v, g, beta = to_chunks(q), to_chunks(k), to_chunks(v), to_chunks(g), to_chunks(beta)
    g = jnp.cumsum(g, axis=-1)
    tril = jnp.tril(jnp.ones((C, C), dtype=bool))
    strict = jnp.tril(jnp.ones((C, C), dtype=bool), -1)
    diff = g[..., :, None] - g[..., None, :]
    decay = jnp.where(tril, jnp.exp(jnp.where(tril, diff, 0.0)), 0.0)
    k_beta = k * beta[..., None]
    v_beta = v * beta[..., None]
    L = jnp.where(strict, jnp.einsum('bnhid,bnhjd->bnhij', k_beta, k) * decay, 0.0)
    eye = jnp.eye(C, dtype=f32)
    t_mat = lax.linalg.triangular_solve(eye + L, jnp.broadcast_to(eye, L.shape),
                                        left_side=True, lower=True, unit_diagonal=True)
    u = t_mat @ v_beta
    w = t_mat @ (k_beta * jnp.exp(g)[..., None])
    intra = jnp.where(tril, jnp.einsum('bnhid,bnhjd->bnhij', q, k) * decay, 0.0)
    q_dec = q * jnp.exp(g)[..., None]
    k_dec = k * jnp.exp(g[..., -1:] - g)[..., None]
    g_last = jnp.exp(g[..., -1])

    def step(S, inp):
        intra_c, qd, kd, u_c, w_c, gl = inp
        v_new = u_c - w_c @ S
        o = qd @ S + intra_c @ v_new
        S = S * gl[..., None, None] + jnp.swapaxes(kd, -1, -2) @ v_new
        return S, o

    xs = (jnp.moveaxis(intra, 1, 0), jnp.moveaxis(q_dec, 1, 0), jnp.moveaxis(k_dec, 1, 0),
          jnp.moveaxis(u, 1, 0), jnp.moveaxis(w, 1, 0), jnp.moveaxis(g_last, 1, 0))
    S0 = jnp.zeros((B, H, Dk, Dv), f32)
    _, o = lax.scan(step, S0, xs)
    o = jnp.swapaxes(jnp.moveaxis(o, 0, 1), 2, 3)
    return o.reshape(B, T, H, Dv)

def peer(h, w_query, sub_keys1, sub_keys2, expert_down, expert_up):
    B, T, D = h.shape
    N = B * T
    hf = h.reshape(N, D)
    qry = (hf @ w_query).reshape(N, PEER_HEADS, 2, PEER_HALF)
    s1 = jnp.einsum('nhc,kc->nhk', qry[:, :, 0], sub_keys1, preferred_element_type=jnp.float32)
    s2 = jnp.einsum('nhc,kc->nhk', qry[:, :, 1], sub_keys2, preferred_element_type=jnp.float32)
    v1, i1 = lax.top_k(s1, PEER_TOPK)
    v2, i2 = lax.top_k(s2, PEER_TOPK)
    cand = (v1[..., :, None] + v2[..., None, :]).reshape(N, PEER_HEADS, PEER_TOPK * PEER_TOPK)
    cand_idx = (i1[..., :, None] * PEER_KEYS + i2[..., None, :]).reshape(
        N, PEER_HEADS, PEER_TOPK * PEER_TOPK)
    top_s, sel = lax.top_k(cand, PEER_TOPK)
    idx = jnp.take_along_axis(cand_idx, sel, axis=-1)
    gates = jax.nn.softmax(top_s, axis=-1)
    hk = PEER_HEADS * PEER_TOPK
    nb = N // PEER_TOKEN_BLOCK

    def block(args):
        xb, ib, gb = args
        u = jnp.take(expert_down, ib, axis=0)
        act = jax.nn.gelu(jnp.einsum('td,tkd->tk', xb, u), approximate=False)
        vsel = jnp.take(expert_up, ib, axis=0)
        return jnp.einsum('tk,tkd->td', (gb * act).astype(xb.dtype), vsel)

    out = lax.map(block, (hf.reshape(nb, PEER_TOKEN_BLOCK, D),
                          idx.reshape(nb, PEER_TOKEN_BLOCK, hk),
                          gates.reshape(nb, PEER_TOKEN_BLOCK, hk)))
    return out.reshape(B, T, D)

def setup_inputs(seed: int = 0):
    key = jax.random.key(seed)
    ks = jax.random.split(key, 17)
    f32 = jnp.float32

    def nrm(k, shape, scale):
        return jax.random.normal(k, shape, f32) * scale

    def gain(k, shape):
        return 1.0 + 0.02 * jax.random.normal(k, shape, f32)

    return {
        'x': nrm(ks[0], (BATCH, SEQ, D_MODEL), 1.0),
        'norm1_w': gain(ks[1], (DEPTH, D_MODEL)),
        'w_in': nrm(ks[2], (DEPTH, D_MODEL, IN_W), D_MODEL ** -0.5),
        'att_q_norm': gain(ks[3], (DEPTH, ATT_HEAD_DIM)),
        'att_k_norm': gain(ks[4], (DEPTH, ATT_HEAD_DIM)),
        'att_sinks': nrm(ks[5], (DEPTH, ATT_HEADS), 0.5),
        'dn_conv_w': nrm(ks[6], (DEPTH, DN_CONV, DN_QKV_W), DN_CONV ** -0.5),
        'dn_A_log': jnp.log(jax.random.uniform(ks[7], (DEPTH, DN_HEADS), f32, 1.0, 16.0)),
        'dn_dt_bias': 1.0 + 0.1 * jax.random.normal(ks[8], (DEPTH, DN_HEADS), f32),
        'dn_out_norm': gain(ks[9], (DEPTH, DN_VAL_DIM)),
        'w_out': nrm(ks[10], (DEPTH, MIX_W, D_MODEL), MIX_W ** -0.5),
        'norm2_w': gain(ks[11], (DEPTH, D_MODEL)),
        'peer_w_query': nrm(ks[12], (DEPTH, D_MODEL, PEER_HEADS * PEER_QDIM), D_MODEL ** -0.5),
        'peer_sub_keys1': nrm(ks[13], (DEPTH, PEER_KEYS, PEER_HALF), PEER_HALF ** -0.5),
        'peer_sub_keys2': nrm(ks[14], (DEPTH, PEER_KEYS, PEER_HALF), PEER_HALF ** -0.5),
        'peer_expert_down': nrm(ks[15], (DEPTH, PEER_EXPERTS, D_MODEL), D_MODEL ** -0.5),
        'peer_expert_up': nrm(ks[16], (DEPTH, PEER_EXPERTS, D_MODEL), PEER_HEADS ** -0.5),
    }

def reference(x, norm1_w, w_in, att_q_norm, att_k_norm, att_sinks, dn_conv_w, dn_A_log,
              dn_dt_bias, dn_out_norm, w_out, norm2_w, peer_w_query, peer_sub_keys1,
              peer_sub_keys2, peer_expert_down, peer_expert_up):
    B, T, _ = x.shape
    pos = jnp.arange(T)
    for l in range(DEPTH):
        h = rms_norm(x, norm1_w[l])
        proj = h @ w_in[l]
        a_q, a_k, a_v, d_qkv, d_gate, d_b, d_a = jnp.split(proj, IN_SPLITS, axis=-1)

        q = a_q.reshape(B, T, ATT_HEADS, ATT_HEAD_DIM)
        k = a_k.reshape(B, T, ATT_KV_HEADS, ATT_HEAD_DIM)
        v = a_v.reshape(B, T, ATT_KV_HEADS, ATT_HEAD_DIM)
        q = partial_rope(rms_norm(q, att_q_norm[l]), pos)
        k = partial_rope(rms_norm(k, att_k_norm[l]), pos)
        att_out = sliding_window_sink_attention(q, k, v, att_sinks[l])

        d_qkv = causal_silu_conv(d_qkv, dn_conv_w[l])
        dq, dk, dv = jnp.split(d_qkv, (DN_QK_W, 2 * DN_QK_W), axis=-1)
        beta = jax.nn.sigmoid(d_b.astype(jnp.float32))
        g = -jnp.exp(dn_A_log[l].astype(jnp.float32)) * jax.nn.softplus(
            d_a.astype(jnp.float32) + dn_dt_bias[l].astype(jnp.float32))
        o = chunk_gated_delta_rule(dq.reshape(B, T, DN_HEADS, DN_KEY_DIM),
                                   dk.reshape(B, T, DN_HEADS, DN_KEY_DIM),
                                   dv.reshape(B, T, DN_HEADS, DN_VAL_DIM), g, beta)
        o = rms_norm(o, dn_out_norm[l]) * jax.nn.silu(
            d_gate.reshape(B, T, DN_HEADS, DN_VAL_DIM).astype(jnp.float32))
        dn_out = o.reshape(B, T, DN_V_W).astype(x.dtype)

        x = x + jnp.concatenate([att_out, dn_out], axis=-1) @ w_out[l]

        x = x + peer(rms_norm(x, norm2_w[l]), peer_w_query[l], peer_sub_keys1[l],
                     peer_sub_keys2[l], peer_expert_down[l], peer_expert_up[l])
    return x


_drawn_inputs = setup_inputs


def setup_inputs(seed=0):
    import zlib

    import numpy as np

    out = dict(_drawn_inputs(seed))
    spreads = {}
    factors = {'att_q_norm': 6.416,
     'att_k_norm': 6.986,
     'att_sinks': 200.0,
     'dn_dt_bias': 37.891,
     'dn_out_norm': 9.298,
     'dn_A_log': 4.795,
     'norm2_w': 9.699}
    for name, (base, spread) in spreads.items():
        noise = np.random.default_rng([zlib.crc32(name.encode()), seed]).standard_normal(out[name].shape)
        drawn = base * np.exp(spread * noise) if base else spread * noise
        out[name] = jnp.asarray(drawn.astype(out[name].dtype))
    for name, factor in factors.items():
        out[name] = (out[name] * factor).astype(out[name].dtype)
    return out
```

```python
from contextlib import ExitStack

import numpy as np
import concourse.bass as bass
from concourse import mybir

F32 = mybir.dt.float32
U32 = mybir.dt.uint32
ALU = mybir.AluOpType
ACT = mybir.ActivationFunctionType
AX = mybir.AxisListType

P = 128
SEQ, D = 1024, 1024
TILES, KT = SEQ // P, D // P
AH, KVH, HD, ROPE = 8, 2, 64, 16
DH, DK, CONV = 4, 128, 4
QK_W = (AH + KVH) * HD
DN0 = QK_W + KVH * HD
GATE0 = DN0 + 3 * DH * DK
BETA0 = GATE0 + DH * DK
IN_W = BETA0 + 2 * DH
CH = 512
N_IN, N_OUT, N_QRY = -(-IN_W // CH), D // CH, 4
CHUNKS = N_IN + N_OUT + N_QRY
PH, NKEY, TOPK = 8, 128, 16
SLOTS = PH * TOPK
EPS = 1e-6
LEVELS = 7
RING = 8
NW = 2
DIAGS = 4
NEG = -1e30
R_QK, R_DT, R_AL, R_SINK, R_DNW, R_N2 = 0, QK_W, QK_W + DH, QK_W + 2 * DH, QK_W + 2 * DH + AH, QK_W + 2 * DH + AH + DK
R_W = R_N2 + D
C_ID, C_ONE, C_TRI, C_LEV = 0, P, 2 * P, 3 * P
C_M0 = C_LEV + LEVELS * P
C_M1 = C_M0 + 2 * P
C_IOTA = C_M1 + 2 * P
C_EPS = C_IOTA + TOPK
C_W = C_EPS + 1
K_N1, K_CONV, K_KEYS = 0, KT, KT + CONV * 12
K_W = K_KEYS + 2 * NKEY

SEG_SLOTS = [4, 6, 6, 6, 6, 6, 6, 4, 4] + [4] * LEVELS + [4, 6, 6, 4, 8, 6, 4, 4, 4, 6]

assert sum(SEG_SLOTS) == SLOTS and all(n % 2 == 0 for n in SEG_SLOTS)


class Steps:

    def __init__(self, sem, n):
        self.sem, self.n = sem, n

    def upto(self, t, k):
        return t * self.n + k


def chunk_cols(c):
    return min(CH, IN_W - c * CH) if c < N_IN else CH


def build(nc, x_rope, weights, experts, rows, cols, consts, out):
    with ExitStack() as ctx:
        def sb(name, shape, dt=F32):
            return ctx.enter_context(nc.sbuf_tensor(name, shape, dt))

        def sem(name):
            return ctx.enter_context(nc.semaphore(name))

        def steps(name, n):
            return Steps(sem(name), n)

        ring = sb("ring", [P, RING, 2 * D])
        wring = sb("wring", [P, NW, KT * CH])
        cst = sb("cst", [P, C_W])
        row = sb("row", [P, R_W])
        col = sb("col", [P, K_W])
        xt = sb("xt", [P, D + ROPE])
        hT = sb("hT", [P, KT, P])
        proj = sb("proj", [P, IN_W])
        qT = sb("qT", [P, AH // 2, P])
        kTw = sb("kTw", [P, 2 * P])
        v2 = sb("v2", [P, 2, P])
        bufA = sb("bufA", [P, 2048])
        bufB = sb("bufB", [P, 2048])
        st = sb("st", [P, 96])
        gs = sb("gs", [P, 24, DH])
        cin = sb("cin", [P, 12, CONV - 1 + P])
        ya = sb("ya", [P, 12, P])
        yb = sb("yb", [P, 12, P])
        state = sb("state", [P, DH, P])
        mix = sb("mix", [P, D])
        x2 = sb("x2", [P, D])
        h2 = sb("h2", [P, D])
        x2c = sb("x2c", [P, D])
        h2c = sb("h2c", [P, D])
        v16 = sb("v16", [P, 2 * PH, TOPK])
        i16 = sb("i16", [P, 2 * PH, TOPK], U32)
        i16f = sb("i16f", [P, 2 * PH, TOPK])
        top = sb("top", [P, PH, TOPK])
        sel = sb("sel", [P, PH, TOPK], U32)
        sab = sb("sab", [P, 2, SLOTS], U32)
        sabf = sb("sabf", [P, 2, SLOTS])
        pick = sb("pick", [P, 2, SLOTS])
        gates = sb("gates", [P, PH, TOPK])
        gsum = sb("gsum", [P, 2, PH])
        idx = sb("idx", [P, SLOTS], U32)
        idxc = sb("idxc", [P, SLOTS], U32)
        gatesc = sb("gatesc", [P, SLOTS])
        dots = sb("dots", [P, SLOTS])
        act_s = sb("act_s", [P, SLOTS])
        wgt = sb("wgt", [P, SLOTS])
        diag = sb("diag", [P, DIAGS, P])
        W = ctx.enter_context(nc.psum_tensor("W", [P, 6, 512], F32))
        acc = ctx.enter_context(nc.psum_tensor("acc", [P, 2, 512], F32))

        ident, ones, tri = (cst[:, c:c + P] for c in (C_ID, C_ONE, C_TRI))
        levels = cst[:, C_LEV:C_LEV + LEVELS * P].rearrange("p (l i) -> p l i", l=LEVELS)
        iota16 = cst[:, C_IOTA:C_IOTA + TOPK]
        eps = cst[:, C_EPS:C_EPS + 1]
        norm1 = col[:, K_N1:K_N1 + KT]
        convw = col[:, K_CONV:K_CONV + CONV * 12].rearrange("p (i b) -> p i b", i=CONV)
        keysT = col[:, K_KEYS:K_KEYS + 2 * NKEY].rearrange("p (s k) -> p s k", s=2)
        sinks = row[:, R_SINK:R_SINK + AH]
        dn_w = row[:, R_DNW:R_DNW + DK]
        norm2 = row[:, R_N2:R_N2 + D]
        h = bufA[:, 0:D]
        bA = bufA[:, :].rearrange("p (n h i) -> p n h i", n=4, h=DH)
        bB = bufB[:, :].rearrange("p (n h i) -> p n h i", n=4, h=DH)
        dg, db, lt, yy = (bA[:, n] for n in range(4))
        inv, invT = bA[:, 0], bA[:, 1]
        ks_s, vtok, rr, vn = (bB[:, n] for n in range(4))
        vb = vtok
        yflat = yb[:, :, :].rearrange("p n i -> p (n i)")
        qk = yflat[:, 0:QK_W]
        qk2 = yflat[:, QK_W:2 * QK_W].rearrange("p (n d) -> p n d", d=HD)
        rope_c = yflat[:, 2 * QK_W:2 * QK_W + 160].rearrange("p (n s e) -> p n s e", s=2, e=8)
        rope_s = ya[:, 0:2, 0:80].rearrange("p s (n e) -> p n s e", e=8)
        qs_s, ktok, o_sq = yb[:, 0:4, :], yb[:, 4:8, :], yb[:, 8:12, :]
        kd = ktok
        o_dn = ya[:, 0:4, :]
        dec = proj[:, 0:512].rearrange("p (h i) -> p h i", h=DH)
        lm = proj[:, DN0:DN0 + 1024].rearrange("p (n h i) -> p n h i", n=2, h=DH)
        intra = proj[:, DN0 + 1024:DN0 + 1536].rearrange("p (h i) -> p h i", h=DH)
        sc2 = proj[:, 0:2048].rearrange("p (n k) -> p n k", k=NKEY)
        out_sb = mix

        def bank(b, n=4):
            return W[:, b, :].rearrange("p (n i) -> p n i", n=n)

        def flat(ap):
            return ap.rearrange("p a b -> p (a b)")

        def over_last(ap, n):
            return ap.unsqueeze(2).broadcast_to([P, ap.shape[1], n])

        def over_mid(ap, n):
            return ap.unsqueeze(1).broadcast_to([P, n, ap.shape[1]])

        consts_in = sem("consts_in")
        x_in = sem("x_in")
        w_in = [sem(f"w_in{i}") for i in range(NW)]
        row_in = [sem(f"row_in{i}") for i in range(RING)]
        negA = steps("neg_exp_a", 2)
        cleared = sem("cleared")
        N1 = steps("norm1_step", 6)
        MM = steps("chunk_mm", CHUNKS)
        MV = steps("window_moved", 1)
        EV = steps("chunk_out", N_IN + N_QRY)
        AT = steps("att_step", 19)
        PT = steps("probs_t", 5)
        DN = steps("dn_step", 16)
        GT = steps("gate_step", 21)
        SG = steps("silu_gate", 1)
        CO = steps("core_step", 18)
        LV = steps("level_step", 4 * LEVELS)
        LM = steps("level_mask", LEVELS)
        OU = steps("out_step", 9)
        QT = steps("query_t", 2 * N_QRY)
        SC = steps("key_scores", N_QRY)
        TK = steps("topk_step", 20)
        idx_ready = sem("idx_ready")
        handed = sem("handed")
        dot_done = sem("dot_done")
        gelu_done = sem("gelu_done")
        wgt_done = sem("wgt_done")
        diag_done = sem("diag_done")
        slot_free = sem("slot_free")
        out_ready = sem("out_ready")
        stored = sem("stored")

        block = ctx.enter_context(nc.Block())
        PER_RING = 16 * SLOTS // RING
        PER_W = 16 * CHUNKS // NW

        def interleaved(eng, segments, slots, finish):
            for seg in segments:
                seg(0)
            finish(None, 0)
            with eng.Fori(1, TILES) as t:
                k = 0
                for seg, n in zip(segments, SEG_SLOTS):
                    seg(t)
                    slots(t - 1, k, k + n)
                    k += n
                finish(t - 1, t)
            slots(TILES - 1, 0, SLOTS)
            finish(TILES - 1, None)

        @block.sync
        def _(sp):
            sp.dma_start(cst[:, :], consts).then_inc(consts_in, 16)
            sp.dma_start(row[:, :], rows.broadcast_to([P, R_W])).then_inc(consts_in, 16)
            sp.dma_start(col[:, :], cols).then_inc(consts_in, 16)

            def loads(t):
                tok = slice(0, P) if isinstance(t, int) else bass.ds(t * P, P)
                if not isinstance(t, int):
                    sp.wait_ge(OU.sem, OU.upto(t - 1, 3))
                sp.dma_start(xt[:, :], x_rope[tok, :]).then_inc(x_in, 16)
                for c in range(CHUNKS):
                    if not (isinstance(t, int) and c < NW):
                        sp.wait_ge(MM.sem, MM.upto(t, c - NW + 1))
                    n = chunk_cols(c)
                    sp.dma_start(wring[:, c % NW, 0:KT * n], weights[c, :, 0:KT * n]).then_inc(w_in[c % NW], 16)

            loads(0)
            with sp.Fori(1, TILES) as t:
                loads(t)

        @block.gpsimd
        def _(pool):
            tile_no = pool.alloc_register("tile_no")
            slot_no = pool.alloc_register("slot_no")
            pool.reg_mov(tile_no, 0)
            pool.reg_mov(slot_no, 0)
            with pool.Fori(0, TILES):
                pool.reg_add(tile_no, tile_no, 1)
                pool.wait_ge(consts_in, 48)
                pool.wait_ge(handed, tile_no)
                for k in range(SLOTS):
                    pool.reg_add(slot_no, slot_no, 1)
                    pool.wait_ge(consts_in, 48)
                    pool.wait_ge(slot_free, slot_no)
                    pool.indirect_dma_start(
                        out=ring[:, k % RING, :], out_offset=None, in_=experts,
                        in_offset=bass.IndirectOffsetOnAxis(ap=idxc[:, k:k + 1], axis=0),
                    ).then_inc(row_in[k % RING], 16)

        @block.tensor
        def _(pe):
            pe.wait_ge(consts_in, 48)
            pe.sem_inc(slot_free, RING)

            def chunk(t, c, dst, src):
                pe.wait_ge(w_in[c % NW], t * PER_W + 16 * (c // NW + 1))
                n = chunk_cols(c)
                wc = wring[:, c % NW, 0:KT * n].rearrange("p (k n) -> p k n", k=KT)
                for k in range(KT):
                    last = pe.matmul(dst[:, 0:n], src[:, k, :], wc[:, k, :], start=k == 0, stop=k == KT - 1)
                last.then_inc(MM.sem, 1)

            def transposes(dst, blocks):
                for j, b in enumerate(blocks):
                    last = pe.transpose(dst[:, j, :], b, ident)
                return last

            def norm1_seg(t):
                if not isinstance(t, int):
                    pe.wait_ge(TK.sem, TK.upto(t - 1, 4))
                pe.wait_ge(N1.sem, N1.upto(t, 4))
                transposes(bank(0), [h[:, P * j:P * j + P] for j in range(4)])
                transposes(bank(1), [h[:, P * j:P * j + P] for j in range(4, 8)]).then_inc(N1.sem, 1)

            def proj_a(t):
                pe.wait_ge(N1.sem, N1.upto(t, 6))
                for c in range(3):
                    chunk(t, c, W[:, 2 + c, :], hT)

            def proj_b(t):
                for c in range(3, N_IN):
                    if c >= 4:
                        pe.wait_ge(EV.sem, EV.upto(t, c - 3))
                    chunk(t, c, W[:, 2 + c % 4, :], hT)

            def transpose_seg(t):
                pe.wait_ge(EV.sem, EV.upto(t, N_IN))
                for g in range(3):
                    last = transposes(bank(2 + g), [proj[:, DN0 + P * b:DN0 + P * b + P]
                                                    for b in range(4 * g, 4 * g + 4)])
                last.then_inc(DN.sem, 1)
                pe.wait_ge(AT.sem, AT.upto(t, 8))
                transposes(bank(0), [flat(qk2[:, 2 * j:2 * j + 2, :]) for j in range(4)])
                pe.transpose(W[:, 1, 0:P], flat(qk2[:, AH:AH + KVH, :]), ident).then_inc(AT.sem, 1)

            def scores_seg(t):
                pe.wait_ge(AT.sem, AT.upto(t, 11))
                pe.wait_ge(DN.sem, DN.upto(t, 3))
                for j in range(4):
                    for a in range(2):
                        rows_ = slice(HD * a, HD * a + HD)
                        last = pe.matmul(W[:, 2 + 2 * a + j // 2, 256 * (j % 2):256 * (j % 2) + 256],
                                         qT[rows_, j, :], kTw[rows_, :], start=True, stop=True)
                last.then_inc(AT.sem, 1)

            def pv_seg(t):
                pe.wait_ge(AT.sem, AT.upto(t, 17))
                pr = bufA[:, :].rearrange("p (b n i) -> p b n i", b=4, n=4)
                for b in range(4):
                    last = transposes(bank(2 + b), [pr[:, b, n, :] for n in range(4)])
                last.then_inc(PT.sem, 1)
                pe.wait_ge(PT.sem, PT.upto(t, 3))
                pt = bufB[:, :].rearrange("p (h c i) -> p h c i", h=AH, c=2)
                for hh in range(AH):
                    kv = hh // (AH // KVH)
                    for c in range(2):
                        last = pe.matmul(W[:, 0, HD * hh:HD * hh + HD], pt[:, hh, c, :],
                                         v2[:, c, HD * kv:HD * kv + HD], start=c == 0, stop=c == 1)
                last.then_inc(PT.sem, 1)

            def qk_norm_seg(t):
                pe.wait_ge(DN.sem, DN.upto(t, 11))
                for g in range(2):
                    last = pe.matmul(W[:, 2 + g, :], ones, flat(yb[:, 4 * g:4 * g + 4, :]), start=True, stop=True)
                last.then_inc(DN.sem, 1)
                pe.wait_ge(DN.sem, DN.upto(t, 15))
                transposes(bank(4), [ya[:, 4 + b, :] for b in range(4)])
                transposes(bank(5), [ya[:, 8 + b, :] for b in range(4)]).then_inc(DN.sem, 1)

            def decay_seg(t):
                pe.wait_ge(PT.sem, PT.upto(t, 5))
                pe.wait_ge(GT.sem, GT.upto(t, 14))
                pe.matmul(W[:, 0, 0:DH], tri, gs[:, 13, :], start=True, stop=True).then_inc(GT.sem, 1)
                pe.wait_ge(GT.sem, GT.upto(t, 17))
                pe.matmul(W[:, 0, :], ones, flat(dg), start=True, stop=True)
                pe.matmul(W[:, 1, :], ones, flat(db), start=True, stop=True).then_inc(GT.sem, 1)

            def core_a(t):
                for hh in range(DH):
                    pe.matmul(bank(2)[:, hh, :], ya[:, 4 + hh, :], ya[:, 4 + hh, :], start=True, stop=True)
                for hh in range(DH):
                    last = pe.matmul(bank(3)[:, hh, :], ya[:, 4 + hh, :], ya[:, hh, :], start=True, stop=True)
                last.then_inc(CO.sem, 1)
                pe.wait_ge(DN.sem, DN.upto(t, 16))
                pe.wait_ge(SG.sem, SG.upto(t, 1))
                pe.wait_ge(GT.sem, GT.upto(t, 20))
                if isinstance(t, int):
                    pe.wait_ge(cleared, 4)
                for hh in range(DH):
                    pe.matmul(bank(5)[:, hh, :], ya[:, 4 + hh, :], state[:, hh, :], start=True, stop=True)
                for hh in range(DH):
                    last = pe.matmul(bank(0)[:, hh, :], ya[:, hh, :], state[:, hh, :], start=True, stop=True)
                last.then_inc(CO.sem, 1)

            def level(m):
                def seg(t):
                    pe.wait_ge(LM.sem, LM.upto(t, m + 1))
                    if m:
                        pe.wait_ge(LV.sem, LV.upto(t, 4 * m))
                    else:
                        pe.wait_ge(CO.sem, CO.upto(t, 4))
                    for hh in range(DH):
                        last = pe.matmul(bank(2)[:, hh, :], lm[:, m % 2, hh, :], inv[:, hh, :], start=True, stop=True)
                    last.then_inc(LV.sem, 1)
                    pe.wait_ge(LV.sem, LV.upto(t, 4 * m + 2))
                    for hh in range(DH):
                        last = pe.matmul(bank(4)[:, hh, :], yy[:, hh, :], invT[:, hh, :], start=True, stop=True)
                    if m < LEVELS - 1:
                        for hh in range(DH):
                            last = pe.matmul(bank(3)[:, hh, :], invT[:, hh, :], yy[:, hh, :], start=True, stop=True)
                    last.then_inc(LV.sem, 1)
                return seg

            def core_b(t):
                pe.wait_ge(LV.sem, LV.upto(t, 4 * LEVELS))
                for hh in range(DH):
                    last = pe.matmul(bank(2)[:, hh, :], invT[:, hh, :], rr[:, hh, :], start=True, stop=True)
                last.then_inc(CO.sem, 1)
                pe.wait_ge(CO.sem, CO.upto(t, 8))
                for hh in range(DH):
                    pe.matmul(bank(3)[:, hh, :], intra[:, hh, :], vn[:, hh, :], start=True, stop=True)
                for hh in range(DH):
                    last = pe.matmul(bank(4)[:, hh, :], kd[:, hh, :], vn[:, hh, :], start=True, stop=True)
                last.then_inc(CO.sem, 1)

            def mix_seg(t):
                pe.wait_ge(CO.sem, CO.upto(t, 18))
                transposes(bank(0), [mix[:, P * j:P * j + P] for j in range(4)])
                transposes(bank(1), [mix[:, P * j:P * j + P] for j in range(4, 8)]).then_inc(OU.sem, 1)

            def out_seg(t):
                pe.wait_ge(OU.sem, OU.upto(t, 2))
                for c in range(2):
                    chunk(t, N_IN + c, W[:, 2 + c, :], hT)

            def norm2_seg(t):
                pe.wait_ge(OU.sem, OU.upto(t, 7))
                transposes(bank(0), [h2[:, P * j:P * j + P] for j in range(4)])
                transposes(bank(1), [h2[:, P * j:P * j + P] for j in range(4, 8)]).then_inc(OU.sem, 1)

            def query_mm(t):
                pe.wait_ge(OU.sem, OU.upto(t, 9))
                for c in range(N_QRY):
                    chunk(t, N_IN + N_OUT + c, W[:, 2 + c, :], hT)

            def key_seg(t):
                for c in range(N_QRY):
                    pe.wait_ge(EV.sem, EV.upto(t, N_IN + c + 1))
                    if c >= 2:
                        pe.wait_ge(QT.sem, QT.upto(t, 2 * c - 2))
                    transposes(bank(c % 2), [bufA[:, CH * c + P * j:CH * c + P * j + P]
                                             for j in range(4)]).then_inc(QT.sem, 1)
                    pe.wait_ge(QT.sem, QT.upto(t, 2 * c + 2))
                    for j in range(4):
                        last = pe.matmul(W[:, 2 + c, P * j:P * j + P], bufB[:, CH * c + P * j:CH * c + P * j + P],
                                         keysT[:, j % 2, :], start=True, stop=True)
                    last.then_inc(SC.sem, 1)

            def none(t):
                pass

            segments = [norm1_seg, proj_a, proj_b, transpose_seg, scores_seg, pv_seg, qk_norm_seg, decay_seg,
                        core_a] + [level(m) for m in range(LEVELS)] + [
                        core_b, mix_seg, out_seg, norm2_seg, query_mm, key_seg, none, none, none, none]

            def slots(u, k0, k1):
                if k0 == 0:
                    pe.wait_ge(handed, u + 1)
                for k in range(k0, k1):
                    pe.wait_ge(diag_done, u * SLOTS + k + 1)
                    for c in range(2):
                        last = pe.matmul(acc[:, c, :], diag[:, k % DIAGS, :],
                                         ring[:, k % RING, D + CH * c:D + CH * c + CH],
                                         start=k == 0, stop=k == SLOTS - 1)
                    last.then_inc(slot_free, 1)

            interleaved(pe, segments, slots, lambda u, t: None)

        @block.scalar
        def _(act):
            act.wait_ge(consts_in, 48)
            act.activation(gs[:, 23, :], row[:, R_AL:R_AL + DH], ACT.Exp).then_inc(negA.sem, 1)

            def norm1_seg(t):
                if not isinstance(t, int):
                    act.wait_ge(idx_ready, t)
                act.wait_ge(x_in, t * 16 + 16)
                act.activation(h, xt[:, 0:D], ACT.Square, accum_out=st[:, 0:1]).then_inc(N1.sem, 1)
                act.wait_ge(N1.sem, N1.upto(t, 1))
                act.activation(st[:, 1:2], st[:, 0:1], ACT.Sqrt, bias=eps, scale=1.0 / D).then_inc(N1.sem, 1)
                act.wait_ge(N1.sem, N1.upto(t, 3))
                act.activation(h, xt[:, 0:D], ACT.Copy, scale=st[:, 2:3]).then_inc(N1.sem, 1)

            def copy_chunk(t, c, dst, src):
                act.wait_ge(MM.sem, MM.upto(t, c + 1))
                act.copy(dst, src).then_inc(EV.sem, 1)

            def proj_a(t):
                for c in range(2):
                    copy_chunk(t, c, proj[:, CH * c:CH * c + CH], W[:, 2 + c, :])

            def proj_b(t):
                act.wait_ge(EV.sem, EV.upto(t, 2))
                act.activation(h[:, 0:QK_W], proj[:, 0:QK_W], ACT.Square).then_inc(AT.sem, 1)
                act.wait_ge(AT.sem, AT.upto(t, 2))
                act.activation(st[:, 20:30], st[:, 10:20], ACT.Sqrt, bias=eps, scale=1.0 / HD).then_inc(AT.sem, 1)
                for c in range(2, N_IN):
                    n = chunk_cols(c)
                    copy_chunk(t, c, proj[:, CH * c:CH * c + n], W[:, 2 + c % 4, 0:n])

            def transpose_seg(t):
                act.wait_ge(DN.sem, DN.upto(t, 2))
                for g in range(3):
                    last = act.copy(cin[:, 4 * g:4 * g + 4, CONV - 1:], bank(2 + g))
                last.then_inc(DN.sem, 1)
                act.wait_ge(AT.sem, AT.upto(t, 9))
                act.copy(qT[:, :, :], bank(0)).then_inc(AT.sem, 1)

            def scores_seg(t):
                act.wait_ge(AT.sem, AT.upto(t, 16))
                for hh in range(AH):
                    act.activation(bufA[:, 256 * hh:256 * hh + 256], bufA[:, 256 * hh:256 * hh + 256], ACT.Exp,
                                   bias=st[:, 40 + hh:41 + hh], accum_out=st[:, 56 + hh:57 + hh])
                act.activation(st[:, 64:72], st[:, 48:56], ACT.Exp).then_inc(AT.sem, 1)

            def pv_seg(t):
                act.wait_ge(PT.sem, PT.upto(t, 1))
                for b in range(2):
                    last = act.copy(bufB[:, CH * b:CH * b + CH], W[:, 2 + b, :])
                last.then_inc(PT.sem, 1)

            def qk_norm_seg(t):
                act.wait_ge(DN.sem, DN.upto(t, 9))
                act.activation(ya[:, :, :], ya[:, :, :], ACT.Silu).then_inc(DN.sem, 1)
                act.wait_ge(DN.sem, DN.upto(t, 10))
                act.activation(yb[:, 0:8, :], ya[:, 0:8, :], ACT.Square).then_inc(DN.sem, 1)
                act.wait_ge(DN.sem, DN.upto(t, 12))
                act.activation(yb[:, 0:8, :], W[:, 2:4, :].rearrange("p b (n i) -> p (b n) i", n=4), ACT.Sqrt,
                               bias=eps).then_inc(DN.sem, 1)
                act.activation(proj[:, GATE0:BETA0], proj[:, GATE0:BETA0], ACT.Silu)
                act.wait_ge(DN.sem, DN.upto(t, 16))
                act.copy(ktok, bank(4))
                act.copy(vtok, bank(5)).then_inc(SG.sem, 1)

            def decay_seg(t):
                act.wait_ge(GT.sem, GT.upto(t, 3))
                act.activation(gs[:, 3, :], gs[:, 2, :], ACT.Exp)
                act.activation(gs[:, 4, :], proj[:, BETA0:BETA0 + DH], ACT.Exp, scale=-1.0).then_inc(GT.sem, 1)
                act.wait_ge(GT.sem, GT.upto(t, 6))
                act.activation(gs[:, 8, :], gs[:, 5, :], ACT.Ln).then_inc(GT.sem, 1)
                act.wait_ge(GT.sem, GT.upto(t, 20))
                act.activation(dec, dec, ACT.Exp)
                act.activation(gs[:, 17:20, :], gs[:, 14:17, :], ACT.Exp).then_inc(GT.sem, 1)

            def none(t):
                pass

            def level(m):
                def seg(t):
                    act.wait_ge(LV.sem, LV.upto(t, 4 * m + 1))
                    act.copy(yy[:, :, :], bank(2)).then_inc(LV.sem, 1)
                return seg

            def core_b(t):
                act.wait_ge(CO.sem, CO.upto(t, 7))
                act.copy(vn[:, :, :], bank(2)).then_inc(CO.sem, 1)
                act.wait_ge(CO.sem, CO.upto(t, 11))
                act.activation(o_sq, o_dn, ACT.Square).then_inc(CO.sem, 1)
                act.wait_ge(CO.sem, CO.upto(t, 13))
                act.activation(gs[:, 21, :], gs[:, 20, :], ACT.Sqrt, bias=eps, scale=1.0 / DK).then_inc(CO.sem, 1)

            def mix_seg(t):
                act.wait_ge(OU.sem, OU.upto(t, 1))
                for g in range(2):
                    last = act.copy(hT[:, 4 * g:4 * g + 4, :], bank(g))
                last.then_inc(OU.sem, 1)

            def norm2_seg(t):
                act.wait_ge(OU.sem, OU.upto(t, 3))
                act.activation(h, x2[:, :], ACT.Square, accum_out=st[:, 80:81]).then_inc(OU.sem, 1)
                act.wait_ge(OU.sem, OU.upto(t, 4))
                act.activation(st[:, 81:82], st[:, 80:81], ACT.Sqrt, bias=eps, scale=1.0 / D).then_inc(OU.sem, 1)
                act.wait_ge(OU.sem, OU.upto(t, 8))
                for g in range(2):
                    last = act.copy(hT[:, 4 * g:4 * g + 4, :], bank(g))
                last.then_inc(OU.sem, 1)

            def query_out(t):
                for c in range(N_QRY):
                    copy_chunk(t, N_IN + N_OUT + c, bufA[:, CH * c:CH * c + CH], W[:, 2 + c, :])

            def key_seg(t):
                for c in range(N_QRY):
                    act.wait_ge(QT.sem, QT.upto(t, 2 * c + 1))
                    act.copy(bufB[:, CH * c:CH * c + CH], W[:, c % 2, :]).then_inc(QT.sem, 1)

            def gate_exp(t):
                act.wait_ge(TK.sem, TK.upto(t, 10))
                act.activation(gates[:, :, :], gates[:, :, :], ACT.Exp).then_inc(TK.sem, 1)

            segments = [norm1_seg, proj_a, proj_b, transpose_seg, scores_seg, pv_seg, qk_norm_seg, decay_seg,
                        none] + [level(m) for m in range(LEVELS)] + [
                        core_b, mix_seg, none, norm2_seg, query_out, key_seg, none, none, gate_exp, none]

            def slots(u, k0, k1):
                for k in range(k0, k1, 2):
                    act.wait_ge(dot_done, u * SLOTS + k + 2)
                    act.activation(act_s[:, k:k + 2], dots[:, k:k + 2], ACT.Gelu).then_inc(gelu_done, 1)
                    act.wait_ge(gelu_done, u * (SLOTS // 2) + k // 2 + 1)
                    for j in (k, k + 1):
                        act.activation(wgt[:, j:j + 1], act_s[:, j:j + 1], ACT.Copy,
                                       scale=gatesc[:, j:j + 1]).then_inc(wgt_done, 1)
                    act.wait_ge(wgt_done, u * SLOTS + k + 2)
                    for j in (k, k + 1):
                        act.wait_ge(slot_free, u * SLOTS + RING + j - DIAGS + 1)
                        act.activation(diag[:, j % DIAGS, :], ident, ACT.Copy,
                                       scale=wgt[:, j:j + 1]).then_inc(diag_done, 1)

            def finish(u, t):
                if u is None:
                    return
                tok = slice(u * P, u * P + P) if isinstance(u, int) else bass.ds(u * P, P)
                act.wait_ge(out_ready, u + 1)
                act.dma_start(out[tok, :], out_sb[:, :]).then_inc(stored, 16)
                act.wait_ge(stored, u * 16 + 16)

            interleaved(act, segments, slots, finish)

        @block.vector
        def _(dve):
            level_reg = dve.alloc_register("level_reg")

            def wait_before_max(stage, t, k):
                if isinstance(t, int):
                    dve.wait_ge(stage.sem, stage.upto(t, k))
                    return
                dve.reg_mul(level_reg, t, stage.n)
                dve.reg_add(level_reg, level_reg, k)
                dve.wait_ge(consts_in, 48)
                dve.wait_ge(stage.sem, level_reg)

            dve.memset(kTw[:, :], 0.0).then_inc(cleared, 1)
            dve.memset(v2[:, :, :], 0.0).then_inc(cleared, 1)
            dve.memset(cin[:, :, :], 0.0).then_inc(cleared, 1)
            dve.memset(state[:, :, :], 0.0).then_inc(cleared, 1)
            dve.wait_ge(consts_in, 48)
            dve.wait_ge(negA.sem, 1)
            dve.tensor_scalar(gs[:, 22, :], gs[:, 23, :], -1.0, None, ALU.mult).then_inc(negA.sem, 1)
            dve.wait_ge(negA.sem, 2)
            dve.wait_ge(cleared, 4)

            def norm1_seg(t):
                dve.wait_ge(N1.sem, N1.upto(t, 2))
                dve.reciprocal(st[:, 2:3], st[:, 1:2]).then_inc(N1.sem, 1)
                dve.wait_ge(N1.sem, N1.upto(t, 5))
                for g in range(2):
                    last = dve.tensor_tensor(hT[:, 4 * g:4 * g + 4, :], bank(g),
                                             over_last(norm1[:, 4 * g:4 * g + 4], P), ALU.mult)
                last.then_inc(N1.sem, 1)

            def none(t):
                pass

            def qk_seg(t):
                dve.wait_ge(AT.sem, AT.upto(t, 1))
                dve.tensor_reduce(st[:, 10:20], h[:, 0:QK_W].rearrange("p (n d) -> p n d", d=HD), AX.X,
                                  ALU.add).then_inc(AT.sem, 1)
                dve.wait_ge(AT.sem, AT.upto(t, 3))
                dve.reciprocal(st[:, 30:40], st[:, 20:30]).then_inc(AT.sem, 1)
                dve.wait_ge(AT.sem, AT.upto(t, 4))
                qk3 = qk.rearrange("p (n d) -> p n d", d=HD)
                dve.tensor_tensor(qk3, proj[:, 0:QK_W].rearrange("p (n d) -> p n d", d=HD),
                                  over_last(st[:, 30:40], HD), ALU.mult).then_inc(AT.sem, 1)
                dve.wait_ge(AT.sem, AT.upto(t, 5))
                for a in range(2):
                    dve.tensor_tensor(qk2[:, 0:AH, :].rearrange("p (j a) d -> p a j d", a=2)[:, a],
                                      qk3[:, 4 * a:4 * a + 4, :],
                                      row[:, R_QK:R_QK + 256].rearrange("p (n d) -> p n d", d=HD), ALU.mult)
                dve.tensor_tensor(qk2[:, AH:, :], qk3[:, AH:, :],
                                  row[:, R_QK + 512:R_QK + QK_W].rearrange("p (n d) -> p n d", d=HD),
                                  ALU.mult).then_inc(AT.sem, 1)
                dve.wait_ge(AT.sem, AT.upto(t, 6))
                x12 = qk2[:, :, 0:ROPE].rearrange("p n (s e) -> p n s e", s=2)
                for dst, c0 in ((rope_c, D), (rope_s, D + 8)):
                    for s in range(2):
                        last = dve.tensor_tensor(dst[:, :, s, :], x12[:, :, s, :],
                                                 over_mid(xt[:, c0:c0 + 8], AH + KVH), ALU.mult)
                last.then_inc(AT.sem, 1)
                dve.wait_ge(AT.sem, AT.upto(t, 7))
                dve.tensor_tensor(x12[:, :, 0, :], rope_c[:, :, 0, :], rope_s[:, :, 1, :], ALU.subtract)
                dve.tensor_tensor(x12[:, :, 1, :], rope_c[:, :, 1, :], rope_s[:, :, 0, :],
                                  ALU.add).then_inc(AT.sem, 1)

            def transpose_seg(t):
                dve.wait_ge(EV.sem, EV.upto(t, N_IN))
                dve.tensor_copy(v2[:, 0, :], v2[:, 1, :])
                dve.tensor_copy(kTw[:, 0:P], kTw[:, P:2 * P]).then_inc(MV.sem, 1)
                dve.tensor_copy(cin[:, :, 0:CONV - 1], cin[:, :, P:P + CONV - 1]).then_inc(DN.sem, 1)
                dve.wait_ge(MV.sem, MV.upto(t, 1))
                dve.tensor_copy(v2[:, 1, :], proj[:, QK_W:QK_W + P])
                dve.wait_ge(AT.sem, AT.upto(t, 9))
                dve.tensor_copy(kTw[:, P:2 * P], W[:, 1, 0:P]).then_inc(AT.sem, 1)

            def softmax_seg(t):
                c0 = C_M0 if isinstance(t, int) else C_M1
                s3 = bufA[:, :].rearrange("p (n k) -> p n k", n=AH)
                dve.wait_ge(AT.sem, AT.upto(t, 12))
                for b in range(4):
                    last = dve.scalar_tensor_tensor(
                        out=s3[:, 2 * b:2 * b + 2, :], in0=bank(2 + b, 2), scalar=HD ** -0.5,
                        in1=over_mid(cst[:, c0:c0 + 2 * P], 2), op0=ALU.mult, op1=ALU.add)
                last.then_inc(AT.sem, 1)
                dve.wait_ge(AT.sem, AT.upto(t, 13))
                dve.tensor_reduce(st[:, 72:80], s3, AX.X, ALU.max).then_inc(AT.sem, 1)
                dve.wait_ge(AT.sem, AT.upto(t, 14))
                dve.tensor_tensor(st[:, 72:80], st[:, 72:80], sinks, ALU.max).then_inc(AT.sem, 1)
                dve.wait_ge(AT.sem, AT.upto(t, 15))
                dve.tensor_scalar(st[:, 40:48], st[:, 72:80], -1.0, None, ALU.mult)
                dve.tensor_tensor(st[:, 48:56], sinks, st[:, 72:80], ALU.subtract).then_inc(AT.sem, 1)
                dve.wait_ge(AT.sem, AT.upto(t, 17))
                dve.tensor_tensor(st[:, 84:92], st[:, 56:64], st[:, 64:72], ALU.add).then_inc(AT.sem, 1)
                dve.wait_ge(AT.sem, AT.upto(t, 18))
                dve.reciprocal(st[:, 72:80], st[:, 84:92]).then_inc(AT.sem, 1)

            def conv_seg(t):
                dve.wait_ge(PT.sem, PT.upto(t, 1))
                for b in range(2, 4):
                    last = dve.tensor_copy(bufB[:, CH * b:CH * b + CH], W[:, 2 + b, :])
                last.then_inc(PT.sem, 1)

                def tap(dst, i):
                    return dve.tensor_tensor(dst[:, :, :], cin[:, :, i:i + P], over_last(convw[:, i, :], P), ALU.mult)

                dve.wait_ge(DN.sem, DN.upto(t, 3))
                tap(ya, 0)
                tap(yb, 1).then_inc(DN.sem, 1)
                for i in range(2, CONV + 1):
                    dve.wait_ge(DN.sem, DN.upto(t, 2 * i))
                    dve.tensor_tensor(ya[:, :, :], ya[:, :, :], yb[:, :, :], ALU.add).then_inc(DN.sem, 1)
                    if i < CONV:
                        dve.wait_ge(DN.sem, DN.upto(t, 2 * i + 1))
                        tap(yb, i).then_inc(DN.sem, 1)
                dve.wait_ge(AT.sem, AT.upto(t, 19))
                dve.wait_ge(PT.sem, PT.upto(t, 4))
                dve.tensor_tensor(mix[:, 0:512].rearrange("p (n d) -> p n d", d=HD), bank(0, AH),
                                  over_last(st[:, 72:80], HD), ALU.mult).then_inc(PT.sem, 1)

            def qk_norm_seg(t):
                dve.wait_ge(DN.sem, DN.upto(t, 13))
                dve.reciprocal(yb[:, 0:8, :], yb[:, 0:8, :]).then_inc(DN.sem, 1)
                dve.wait_ge(DN.sem, DN.upto(t, 14))
                dve.scalar_tensor_tensor(out=ya[:, 0:4, :], in0=yb[:, 0:4, :], scalar=DK ** -0.5, in1=ya[:, 0:4, :],
                                         op0=ALU.mult, op1=ALU.mult)
                dve.tensor_tensor(ya[:, 4:8, :], ya[:, 4:8, :], yb[:, 4:8, :], ALU.mult).then_inc(DN.sem, 1)

            def decay_seg(t):
                def g(n):
                    return gs[:, n, :]

                dve.tensor_tensor(g(0), proj[:, BETA0 + DH:IN_W], row[:, R_DT:R_DT + DH], ALU.add).then_inc(GT.sem, 1)
                dve.wait_ge(GT.sem, GT.upto(t, 1))
                dve.tensor_scalar(g(1), g(0), -1.0, None, ALU.mult).then_inc(GT.sem, 1)
                dve.wait_ge(GT.sem, GT.upto(t, 2))
                dve.tensor_tensor(g(2), g(0), g(1), ALU.min).then_inc(GT.sem, 1)
                dve.wait_ge(GT.sem, GT.upto(t, 4))
                dve.tensor_scalar(g(5), g(3), 1.0, None, ALU.add)
                dve.tensor_scalar(g(6), g(4), 1.0, None, ALU.add).then_inc(GT.sem, 1)
                dve.wait_ge(GT.sem, GT.upto(t, 5))
                dve.reciprocal(g(7), g(6)).then_inc(GT.sem, 1)
                dve.wait_ge(GT.sem, GT.upto(t, 7))
                dve.tensor_scalar(g(9), g(5), -1.0, None, ALU.add)
                dve.tensor_scalar(g(10), g(5), 1.0, None, ALU.is_equal).then_inc(GT.sem, 1)
                dve.wait_ge(GT.sem, GT.upto(t, 8))
                dve.tensor_tensor(g(9), g(9), g(10), ALU.add)
                dve.tensor_tensor(g(8), g(8), g(10), ALU.add).then_inc(GT.sem, 1)
                dve.wait_ge(GT.sem, GT.upto(t, 9))
                dve.reciprocal(g(11), g(9))
                dve.tensor_tensor(g(12), g(8), g(3), ALU.mult).then_inc(GT.sem, 1)
                dve.wait_ge(GT.sem, GT.upto(t, 10))
                dve.tensor_tensor(g(12), g(12), g(11), ALU.mult).then_inc(GT.sem, 1)
                dve.tensor_scalar(g(1), g(0), 0.0, None, ALU.max).then_inc(GT.sem, 1)
                dve.wait_ge(GT.sem, GT.upto(t, 12))
                dve.tensor_tensor(g(12), g(12), g(1), ALU.add).then_inc(GT.sem, 1)
                dve.wait_ge(GT.sem, GT.upto(t, 13))
                dve.tensor_tensor(g(13), g(12), g(22), ALU.mult).then_inc(GT.sem, 1)
                dve.wait_ge(GT.sem, GT.upto(t, 15))
                dve.tensor_copy(g(16), W[:, 0, 0:DH]).then_inc(GT.sem, 1)
                dve.wait_ge(GT.sem, GT.upto(t, 16))
                dve.tensor_tensor(dg, over_mid(ident, DH), over_last(g(16), P), ALU.mult)
                dve.tensor_tensor(db, over_mid(ident, DH), over_last(g(7), P), ALU.mult).then_inc(GT.sem, 1)
                dve.wait_ge(GT.sem, GT.upto(t, 18))
                for hh in range(DH):
                    dve.tensor_scalar(dec[:, hh, :], bank(0)[:, hh, :], gs[:, 16, hh:hh + 1], 0.0,
                                      ALU.subtract, ALU.min)
                dve.tensor_tensor(g(14), bank(0)[:, :, P - 1], g(16), ALU.subtract)
                dve.tensor_copy(g(15), bank(0)[:, :, P - 1]).then_inc(GT.sem, 1)
                dve.wait_ge(GT.sem, GT.upto(t, 19))
                dve.tensor_scalar(g(14), g(14), 0.0, None, ALU.min).then_inc(GT.sem, 1)
                dve.wait_ge(GT.sem, GT.upto(t, 21))
                dve.tensor_tensor(dec, dec, over_mid(tri, DH), ALU.mult)
                dve.tensor_tensor(gs[:, 20, :], g(7), g(19), ALU.mult)

            def masked(t, m):
                return dve.tensor_tensor(lm[:, m % 2], lt, over_mid(levels[:, m, :], DH), ALU.mult)

            def core_a(t):
                dve.wait_ge(CO.sem, CO.upto(t, 2))
                dve.tensor_copy(inv, over_mid(ident, DH))
                dve.tensor_copy(invT, over_mid(ident, DH)).then_inc(CO.sem, 1)
                dve.wait_ge(CO.sem, CO.upto(t, 3))
                dve.tensor_tensor(lt, bank(2), dec, ALU.mult).then_inc(CO.sem, 1)
                dve.tensor_tensor(intra, bank(3), dec, ALU.mult)
                dve.wait_ge(CO.sem, CO.upto(t, 4))
                dve.tensor_tensor(lt, lt, bank(1), ALU.mult).then_inc(CO.sem, 1)
                dve.wait_ge(SG.sem, SG.upto(t, 1))
                dve.tensor_tensor(ks_s, bank(5), over_last(gs[:, 20, :], P), ALU.mult)
                dve.tensor_tensor(vb, vtok, over_last(gs[:, 7, :], P), ALU.mult)
                dve.tensor_tensor(qs_s, bank(0), over_last(gs[:, 19, :], P), ALU.mult)
                dve.wait_ge(CO.sem, CO.upto(t, 5))
                masked(t, 0).then_inc(LM.sem, 1)
                dve.wait_ge(LM.sem, LM.upto(t, 1))
                dve.tensor_tensor(rr, vb, ks_s, ALU.subtract).then_inc(CO.sem, 1)
                dve.tensor_tensor(kd, ktok, over_last(gs[:, 17, :], P), ALU.mult)

            def level(m):
                def seg(t):
                    if m < LEVELS - 1:
                        masked(t, m + 1).then_inc(LM.sem, 1)
                    dve.wait_ge(LV.sem, LV.upto(t, 4 * m + 3))
                    if m < LEVELS - 1:
                        dve.tensor_tensor(inv, inv, bank(3), ALU.subtract)
                    dve.tensor_tensor(invT, invT, bank(4), ALU.subtract).then_inc(LV.sem, 1)
                return seg

            def core_b(t):
                dve.wait_ge(CO.sem, CO.upto(t, 9))
                dve.tensor_tensor(o_dn, qs_s, bank(3), ALU.add)
                dve.tensor_tensor(state[:, :, :], state[:, :, :], over_last(gs[:, 18, :], P),
                                  ALU.mult).then_inc(CO.sem, 1)
                dve.wait_ge(CO.sem, CO.upto(t, 10))
                dve.tensor_tensor(state[:, :, :], state[:, :, :], bank(4), ALU.add).then_inc(CO.sem, 1)
                dve.wait_ge(CO.sem, CO.upto(t, 12))
                dve.tensor_reduce(gs[:, 20, :], o_sq, AX.X, ALU.add).then_inc(CO.sem, 1)
                dve.wait_ge(CO.sem, CO.upto(t, 14))
                dve.reciprocal(gs[:, 20, :], gs[:, 21, :]).then_inc(CO.sem, 1)
                dve.wait_ge(CO.sem, CO.upto(t, 15))
                dve.tensor_tensor(o_dn, o_dn, over_last(gs[:, 20, :], P), ALU.mult).then_inc(CO.sem, 1)
                dve.wait_ge(CO.sem, CO.upto(t, 16))
                dve.tensor_tensor(o_dn, o_dn, over_mid(dn_w, DH), ALU.mult).then_inc(CO.sem, 1)
                dve.wait_ge(CO.sem, CO.upto(t, 17))
                dve.tensor_tensor(mix[:, 512:D], flat(o_dn), proj[:, GATE0:BETA0], ALU.mult).then_inc(CO.sem, 1)

            def out_seg(t):
                dve.wait_ge(MM.sem, MM.upto(t, N_IN + N_OUT))
                dve.tensor_tensor(x2[:, :], xt[:, 0:D], flat(W[:, 2:4, :]), ALU.add).then_inc(OU.sem, 1)

            def norm2_seg(t):
                dve.wait_ge(OU.sem, OU.upto(t, 5))
                dve.reciprocal(st[:, 82:83], st[:, 81:82]).then_inc(OU.sem, 1)
                dve.wait_ge(OU.sem, OU.upto(t, 6))
                dve.scalar_tensor_tensor(out=h2[:, :], in0=x2[:, :], scalar=st[:, 82:83], in1=norm2,
                                         op0=ALU.mult, op1=ALU.mult).then_inc(OU.sem, 1)

            s_in = flat(W[:, 2:6, :]).rearrange("p (n k) -> p n k", k=NKEY)

            def top_a(t):
                for n in range(2 * PH):
                    if n % 4 == 0:
                        wait_before_max(SC, t, n // 4 + 1)
                    last = dve.max(v16[:, n, 0:8], s_in[:, n, :])
                last.then_inc(TK.sem, 1)
                wait_before_max(TK, t, 1)
                for n in range(2 * PH):
                    last = dve.match_replace(sc2[:, n, :], v16[:, n, 0:8], s_in[:, n, :], -3e38)
                last.then_inc(TK.sem, 1)

            def top_b(t):
                wait_before_max(TK, t, 2)
                for n in range(2 * PH):
                    last = dve.max(v16[:, n, 8:16], sc2[:, n, :])
                last.then_inc(TK.sem, 1)
                for n in range(2 * PH):
                    last = dve.max_index(i16[:, n, 0:8], v16[:, n, 0:8], s_in[:, n, :])
                last.then_inc(TK.sem, 1)
                wait_before_max(TK, t, 3)
                for n in range(2 * PH):
                    last = dve.max_index(i16[:, n, 8:16], v16[:, n, 8:16], sc2[:, n, :])
                last.then_inc(TK.sem, 1)

            cand = bufA[:, :].rearrange("p (n a b) -> p n a b", a=TOPK, b=TOPK)
            cand2 = bufA[:, :].rearrange("p (n c) -> p n c", n=PH)
            left = proj[:, 0:2048].rearrange("p (n c) -> p n c", n=PH)
            v_h = v16[:, :, :].rearrange("p (n s) k -> p n s k", s=2)

            def top_c(t):
                dve.wait_ge(TK.sem, TK.upto(t, 5))
                for n in range(PH):
                    last = dve.tensor_tensor(cand[:, n], over_last(v_h[:, n, 0, :], TOPK),
                                             over_mid(v_h[:, n, 1, :], TOPK), ALU.add)
                last.then_inc(TK.sem, 1)
                wait_before_max(TK, t, 6)
                for n in range(PH):
                    last = dve.max(top[:, n, 0:8], cand2[:, n, :])
                last.then_inc(TK.sem, 1)
                wait_before_max(TK, t, 7)
                for n in range(PH):
                    last = dve.match_replace(left[:, n, :], top[:, n, 0:8], cand2[:, n, :], -3e38)
                last.then_inc(TK.sem, 1)

            def top_d(t):
                wait_before_max(TK, t, 8)
                for n in range(PH):
                    last = dve.max(top[:, n, 8:16], left[:, n, :])
                last.then_inc(TK.sem, 1)
                dve.wait_ge(TK.sem, TK.upto(t, 9))
                dve.tensor_tensor(gates[:, :, :], top[:, :, :], over_last(top[:, :, 0], TOPK),
                                  ALU.subtract).then_inc(TK.sem, 1)
                for n in range(PH):
                    dve.max_index(sel[:, n, 0:8], top[:, n, 0:8], cand2[:, n, :])
                for n in range(PH):
                    dve.max_index(sel[:, n, 8:16], top[:, n, 8:16], left[:, n, :])
                dve.wait_ge(TK.sem, TK.upto(t, 11))
                dve.tensor_reduce(gsum[:, 0, :], gates[:, :, :], AX.X, ALU.add).then_inc(TK.sem, 1)
                dve.wait_ge(TK.sem, TK.upto(t, 12))
                dve.reciprocal(gsum[:, 1, :], gsum[:, 0, :])
                dve.tensor_scalar(sab[:, 0, :], flat(sel[:, :, :]), 4, None, ALU.logical_shift_right)
                dve.tensor_scalar(sab[:, 1, :], flat(sel[:, :, :]), TOPK - 1, None, ALU.bitwise_and).then_inc(TK.sem, 1)

            def top_e(t):
                dve.wait_ge(TK.sem, TK.upto(t, 13))
                dve.tensor_tensor(gates[:, :, :], gates[:, :, :], over_last(gsum[:, 1, :], TOPK), ALU.mult)
                dve.tensor_copy(sabf[:, :, :], sab[:, :, :])
                dve.tensor_copy(i16f[:, :, :], i16[:, :, :]).then_inc(TK.sem, 1)
                i_h = i16f[:, :, :].rearrange("p (n s) k -> p n s k", s=2)
                own = bufB[:, :].rearrange("p (m k) -> p m k", k=TOPK)
                for s in range(2):
                    dve.wait_ge(TK.sem, TK.upto(t, 14 + 3 * s))
                    dve.tensor_tensor(own, over_last(sabf[:, s, :], TOPK), over_mid(iota16, SLOTS),
                                      ALU.is_equal).then_inc(TK.sem, 1)
                    dve.wait_ge(TK.sem, TK.upto(t, 15 + 3 * s))
                    for n in range(PH):
                        last = dve.tensor_tensor(own[:, TOPK * n:TOPK * n + TOPK, :], own[:, TOPK * n:TOPK * n + TOPK, :],
                                                 over_mid(i_h[:, n, s, :], TOPK), ALU.mult)
                    last.then_inc(TK.sem, 1)
                    dve.wait_ge(TK.sem, TK.upto(t, 16 + 3 * s))
                    last = dve.tensor_reduce(pick[:, s, :], own, AX.X, ALU.add)
                    last.then_inc(TK.sem, 1)
                dve.wait_ge(TK.sem, TK.upto(t, 20))
                dve.scalar_tensor_tensor(out=idx[:, :], in0=pick[:, 0, :], scalar=float(NKEY), in1=pick[:, 1, :],
                                         op0=ALU.mult, op1=ALU.add).then_inc(idx_ready, 1)

            segments = [norm1_seg, none, qk_seg, transpose_seg, softmax_seg, conv_seg, qk_norm_seg, decay_seg,
                        core_a] + [level(m) for m in range(LEVELS)] + [
                        core_b, none, out_seg, norm2_seg, none, none, top_a, top_b, lambda t: (top_c(t), top_d(t)), top_e]

            def slots(u, k0, k1):
                for k in range(k0, k1):
                    dve.wait_ge(row_in[k % RING], u * PER_RING + 16 * (k // RING + 1))
                    down = ring[:, k % RING, 0:D]
                    dve.tensor_tensor_reduce(out=down, in0=down, in1=h2c[:, :], scale=1.0, scalar=0.0,
                                             op0=ALU.mult, op1=ALU.add, accum_out=dots[:, k:k + 1]).then_inc(dot_done, 1)

            def finish(u, t):
                if u is not None:
                    dve.wait_ge(slot_free, u * SLOTS + RING + SLOTS)
                    dve.tensor_tensor(out_sb[:, :], x2c[:, :], flat(acc[:, :, :]), ALU.add).then_inc(out_ready, 1)
                    dve.wait_ge(out_ready, u + 1)
                if t is not None:
                    dve.wait_ge(idx_ready, t + 1)
                    dve.tensor_copy(idxc[:, :], idx[:, :])
                    dve.tensor_copy(gatesc[:, :], flat(gates[:, :, :]))
                    dve.tensor_copy(x2c[:, :], x2[:, :])
                    dve.tensor_copy(h2c[:, :], h2[:, :]).then_inc(handed, 1)
                    dve.wait_ge(handed, t + 1)

            interleaved(dve, segments, slots, finish)


def kernel(x, norm1_w, w_in, att_q_norm, att_k_norm, att_sinks, dn_conv_w, dn_A_log, dn_dt_bias, dn_out_norm,
           w_out, norm2_w, peer_w_query, peer_sub_keys1, peer_sub_keys2, peer_expert_down, peer_expert_up):
    import concourse.bacc as bacc
    from concourse.bass_utils import run_bass_kernel_spmd

    inv_freq = np.float32(500000.0) ** (-(np.arange(8, dtype=np.float32) * np.float32(2.0) / np.float32(ROPE)))
    ang = np.arange(SEQ, dtype=np.float32)[:, None] * inv_freq[None, :].astype(np.float32)
    i = np.arange(P)
    masks = [((i[None, :] // (2 * s) == i[:, None] // (2 * s)) & ((i[None, :] // s) % 2 == 1)
              & ((i[:, None] // s) % 2 == 0)) for s in (1 << m for m in range(LEVELS))]
    key = np.arange(2 * P)[None, :]
    valid = (key > i[:, None]) & (key <= i[:, None] + P)
    consts = np.concatenate(
        [np.eye(P), np.ones((P, P)), i[None, :] >= i[:, None]] + masks
        + [np.where(valid & (key >= P), 0.0, NEG), np.where(valid, 0.0, NEG),
           np.tile(np.arange(TOPK), (P, 1)), np.full((P, 1), EPS)], axis=1).astype(np.float32)

    def chunks(w):
        out_ = np.zeros((-(-w.shape[1] // CH), P, KT * CH), np.float32)
        for c in range(out_.shape[0]):
            part = w[:, c * CH:(c + 1) * CH]
            n = part.shape[1]
            out_[c, :, :KT * n] = part.reshape(KT, P, n).transpose(1, 0, 2).reshape(P, KT * n)
        return out_

    arrays = {
        "x_rope": np.concatenate([x[0], np.cos(ang), np.sin(ang)], axis=1),
        "weights": np.concatenate([chunks(w_in[0]), chunks(w_out[0]), chunks(peer_w_query[0])]),
        "experts": np.concatenate([peer_expert_down[0], peer_expert_up[0]], axis=1),
        "rows": np.concatenate([np.tile(att_q_norm[0], AH), np.tile(att_k_norm[0], KVH), dn_dt_bias[0], dn_A_log[0],
                                att_sinks[0], dn_out_norm[0], norm2_w[0]])[None, :],
        "cols": np.concatenate([norm1_w[0].reshape(KT, P).T,
                                dn_conv_w[0].reshape(CONV, 12, P).transpose(2, 0, 1).reshape(P, CONV * 12),
                                peer_sub_keys1[0].T, peer_sub_keys2[0].T], axis=1),
        "consts": consts,
    }
    nc = bacc.Bacc("TRN2", target_bir_lowering=False, num_devices=1)
    arrays = {n: np.ascontiguousarray(a) for n, a in arrays.items()}
    aps = [nc.dram_tensor(n, a.shape, mybir.dt.from_np(a.dtype), kind="ExternalInput").ap()
           for n, a in arrays.items()]
    out = nc.dram_tensor("out", (SEQ, D), F32, kind="ExternalOutput").ap()
    build(nc, *aps, out)
    r = run_bass_kernel_spmd(nc, [arrays], core_ids=[0])
    return r.results[0]["out"].reshape(1, SEQ, D)
```

```python
from contextlib import ExitStack

import numpy as np
import concourse.bass as bass
from concourse import mybir

F32 = mybir.dt.float32
U32 = mybir.dt.uint32
ALU = mybir.AluOpType
ACT = mybir.ActivationFunctionType
AX = mybir.AxisListType

P = 128
SEQ, D = 1024, 1024
TILES, KT = SEQ // P, D // P
AH, KVH, HD, ROPE = 8, 2, 64, 16
DH, DK, CONV = 4, 128, 4
QK_W = (AH + KVH) * HD
DN0 = QK_W + KVH * HD
GATE0 = DN0 + 3 * DH * DK
BETA0 = GATE0 + DH * DK
IN_W = BETA0 + 2 * DH
CH = 512
N_IN, N_OUT, N_QRY = -(-IN_W // CH), D // CH, 4
CHUNKS = N_IN + N_OUT + N_QRY
PH, NKEY, TOPK = 8, 128, 16
SLOTS = PH * TOPK
EPS = 1e-6
LEVELS = 7
RING = 8
DOT_LEAD = 8
DIAG_LEAD = 4
HALF = SLOTS // 2
NW = 2
DIAGS = 16
NEG = -1e30
R_QK, R_DT, R_AL, R_SINK, R_DNW, R_N2 = 0, QK_W, QK_W + DH, QK_W + 2 * DH, QK_W + 2 * DH + AH, QK_W + 2 * DH + AH + DK
R_W = R_N2 + D
C_ID, C_ONE, C_TRI, C_LEV = 0, P, 2 * P, 3 * P
C_M0 = C_LEV + LEVELS * P
C_M1 = C_M0 + 2 * P
C_IOTA = C_M1 + 2 * P
C_EPS = C_IOTA + TOPK
C_W = C_EPS + 1
K_N1, K_CONV, K_KEYS = 0, KT, KT + CONV * 12
K_W = K_KEYS + 2 * NKEY

SEG_SLOTS = ([4, 2] + [4] * N_IN + [4, 6, 4, 4, 6, 4] + [2] * LEVELS + [4, 4, 2, 4, 4]
             + [4] * N_QRY + [4, 8, 8, 2])
assert sum(SEG_SLOTS) == SLOTS and all(n % 2 == 0 for n in SEG_SLOTS)


class Steps:

    def __init__(self, sem, n):
        self.sem, self.n = sem, n

    def upto(self, t, k):
        return t * self.n + k


def chunk_cols(c):
    return min(CH, IN_W - c * CH) if c < N_IN else CH


def build(nc, x_rope, weights, experts_down, experts_up, rows, cols, consts, out):
    with ExitStack() as ctx:
        def sb(name, shape, dt=F32):
            return ctx.enter_context(nc.sbuf_tensor(name, shape, dt))

        def sem(name):
            return ctx.enter_context(nc.semaphore(name))

        def steps(name, n):
            return Steps(sem(name), n)

        down_ring = sb("down_ring", [P, RING, D])
        up_ring = sb("up_ring", [P, RING, D])
        wring = sb("wring", [P, NW, KT * CH])
        cst = sb("cst", [P, C_W])
        row = sb("row", [P, R_W])
        col = sb("col", [P, K_W])
        xt = sb("xt", [P, D + ROPE])
        hT = sb("hT", [P, KT, P])
        proj = sb("proj", [P, IN_W])
        qT = sb("qT", [P, AH // 2, P])
        kTw = sb("kTw", [P, 2 * P])
        v2 = sb("v2", [P, 2, P])
        bufA = sb("bufA", [P, 2048])
        bufB = sb("bufB", [P, 2048])
        st = sb("st", [P, 96])
        gs = sb("gs", [P, 24, DH])
        cin = sb("cin", [P, 12, CONV - 1 + P])
        ya = sb("ya", [P, 12, P])
        yb = sb("yb", [P, 12, P])
        state = sb("state", [P, DH, P])
        mix = sb("mix", [P, D])
        x2 = sb("x2", [P, D])
        h2 = sb("h2", [P, D])
        x2c = sb("x2c", [P, D])
        h2c = sb("h2c", [P, D])
        v16 = sb("v16", [P, 2 * PH, TOPK])
        i16 = sb("i16", [P, 2 * PH, TOPK], U32)
        top_s = sb("top_s", [P, PH, TOPK])
        sel = sb("sel", [P, PH, TOPK], U32)
        sab = sb("sab", [P, 2, SLOTS], U32)
        gates = sb("gates", [P, PH, TOPK])
        gsum = sb("gsum", [P, 2, PH])
        idx = sb("idx", [P, SLOTS], U32)
        idxc = sb("idxc", [P, SLOTS], U32)
        idxu = sb("idxu", [P, SLOTS], U32)
        gatesc = sb("gatesc", [P, SLOTS])
        dots = sb("dots", [P, SLOTS])
        act_s = sb("act_s", [P, SLOTS])
        wgt = sb("wgt", [P, SLOTS])
        diag = sb("diag", [P, DIAGS, P])
        W = ctx.enter_context(nc.psum_tensor("W", [P, 6, 512], F32))
        acc = ctx.enter_context(nc.psum_tensor("acc", [P, 2, 512], F32))

        ident, ones, tri = (cst[:, c:c + P] for c in (C_ID, C_ONE, C_TRI))
        levels = cst[:, C_LEV:C_LEV + LEVELS * P].rearrange("p (l i) -> p l i", l=LEVELS)
        iota16 = cst[:, C_IOTA:C_IOTA + TOPK]
        eps = cst[:, C_EPS:C_EPS + 1]
        norm1 = col[:, K_N1:K_N1 + KT]
        convw = col[:, K_CONV:K_CONV + CONV * 12].rearrange("p (i b) -> p i b", i=CONV)
        keysT = col[:, K_KEYS:K_KEYS + 2 * NKEY].rearrange("p (s k) -> p s k", s=2)
        sinks = row[:, R_SINK:R_SINK + AH]
        dn_w = row[:, R_DNW:R_DNW + DK]
        norm2 = row[:, R_N2:R_N2 + D]
        h = bufA[:, 0:D]
        bA = bufA[:, :].rearrange("p (n h i) -> p n h i", n=4, h=DH)
        bB = bufB[:, :].rearrange("p (n h i) -> p n h i", n=4, h=DH)
        dg, db, lt, yy = (bA[:, n] for n in range(4))
        inv, invT = bA[:, 0], bA[:, 1]
        ks_s, vtok, rr, vn = (bB[:, n] for n in range(4))
        vb = vtok
        yflat = yb[:, :, :].rearrange("p n i -> p (n i)")
        qk = yflat[:, 0:QK_W]
        qk2 = yflat[:, QK_W:2 * QK_W].rearrange("p (n d) -> p n d", d=HD)
        rope_c = yflat[:, 2 * QK_W:2 * QK_W + 160].rearrange("p (n s e) -> p n s e", s=2, e=8)
        rope_s = ya[:, 0:2, 0:80].rearrange("p s (n e) -> p n s e", e=8)
        qs_s, ktok, o_sq = yb[:, 0:4, :], yb[:, 4:8, :], yb[:, 8:12, :]
        kd = ktok
        o_dn = ya[:, 0:4, :]
        dec = proj[:, 0:512].rearrange("p (h i) -> p h i", h=DH)
        lm = proj[:, DN0:DN0 + 1024].rearrange("p (n h i) -> p n h i", n=2, h=DH)
        intra = proj[:, DN0 + 1024:DN0 + 1536].rearrange("p (h i) -> p h i", h=DH)
        sabf = mix[:, 0:256].rearrange("p (s m) -> p s m", s=2)
        pick = mix[:, 256:512].rearrange("p (s m) -> p s m", s=2)
        i16f = mix[:, 512:768].rearrange("p (n k) -> p n k", k=TOPK)
        out_sb = mix

        def bank(b, n=4):
            return W[:, b, :].rearrange("p (n i) -> p n i", n=n)

        def flat(ap):
            return ap.rearrange("p a b -> p (a b)")

        def over_last(ap, n):
            return ap.unsqueeze(2).broadcast_to([P, ap.shape[1], n])

        def over_mid(ap, n):
            return ap.unsqueeze(1).broadcast_to([P, n, ap.shape[1]])

        consts_in = sem("consts_in")
        x_in = sem("x_in")
        w_in = [sem(f"w_in{i}") for i in range(NW)]
        down_in = [sem(f"down_in{i}") for i in range(RING)]
        up_in = [sem(f"up_in{i}") for i in range(RING)]
        negA = steps("neg_exp_a", 2)
        cleared = sem("cleared")
        N1 = steps("norm1_step", 6)
        MM = steps("chunk_mm", CHUNKS)
        MV = steps("window_moved", 1)
        EV = steps("chunk_out", N_IN + N_QRY)
        AT = steps("att_step", 19)
        PT = steps("probs_t", 5)
        DN = steps("dn_step", 16)
        GT = steps("gate_step", 21)
        SG = steps("silu_gate", 1)
        CO = steps("core_step", 18)
        LV = steps("level_step", 4 * LEVELS)
        LM = steps("level_mask", LEVELS)
        OU = steps("out_step", 9)
        QT = steps("query_t", 2 * N_QRY)
        SC = steps("key_scores", N_QRY)
        TK = steps("topk_step", 15 * N_QRY)
        SM = steps("gate_softmax", 4)
        idx_ready = sem("idx_ready")
        handed = sem("handed")
        handed_late = sem("handed_late")
        down_free = sem("down_free")
        gelu_done = sem("gelu_done")
        wgt_done = sem("wgt_done")
        diag_done = sem("diag_done")
        up_free = sem("up_free")
        out_ready = sem("out_ready")
        stored = sem("stored")

        block = ctx.enter_context(nc.Block())
        PER_RING = 16 * SLOTS // RING
        PER_W = 16 * CHUNKS // NW

        def interleaved(eng, segments, slots, lead=0, hand=lambda t: None, final=lambda u, t: None):
            assert len(segments) == len(SEG_SLOTS)
            for seg in segments:
                seg(0)
            hand(0)
            slots(0, 0, lead)
            final(None, 0)
            with eng.Fori(1, TILES) as t:
                k = lead
                for seg, n in zip(segments, SEG_SLOTS):
                    seg(t)
                    slots(t - 1, min(k, SLOTS), min(k + n, SLOTS))
                    k += n
                hand(t)
                slots(t, 0, lead)
                final(t - 1, t)
            slots(TILES - 1, lead, SLOTS)
            final(TILES - 1, None)

        @block.sync
        def _(sp):
            sp.dma_start(cst[:, :], consts).then_inc(consts_in, 16)
            sp.dma_start(row[:, :], rows.broadcast_to([P, R_W])).then_inc(consts_in, 16)
            sp.dma_start(col[:, :], cols).then_inc(consts_in, 16)

            counted = sp.alloc_register("counted")

            def wait_apart(sem_, t, n, k):
                if isinstance(t, int):
                    sp.wait_ge(sem_, t * n + k)
                    return
                sp.reg_mul(counted, t, n)
                sp.reg_add(counted, counted, k)
                sp.wait_ge(consts_in, 48)
                sp.wait_ge(sem_, counted)

            def load_x(t):
                tok = slice(t * P, t * P + P) if isinstance(t, int) else bass.ds(t * P, P)
                sp.dma_start(xt[:, :], x_rope[tok, :]).then_inc(x_in, 16)

            def load_chunks(t, chunks, first=False):
                for c in chunks:
                    if not first:
                        sp.wait_ge(MM.sem, MM.upto(t, c - NW + 1))
                    n = chunk_cols(c)
                    sp.dma_start(wring[:, c % NW, 0:KT * n], weights[c, :, 0:KT * n]).then_inc(w_in[c % NW], 16)

            def next_tile(t):
                wait_apart(OU.sem, t, OU.n, 3)
                load_x(t + 1)
                load_chunks(t + 1, range(NW))

            def store_before(t):
                u = t - 1
                tok = slice(u * P, u * P + P) if isinstance(u, int) else bass.ds(u * P, P)
                wait_apart(out_ready, t, 1, 0)
                sp.dma_start(out[tok, :], out_sb[:, :]).then_inc(stored, 16)
                wait_apart(stored, t, 16, 0)

            load_x(0)
            load_chunks(0, range(NW), first=True)
            load_chunks(0, range(NW, CHUNKS))
            next_tile(0)
            with sp.Fori(1, TILES - 1) as t:
                load_chunks(t, range(NW, CHUNKS))
                next_tile(t)
                store_before(t)
            load_chunks(TILES - 1, range(NW, CHUNKS))
            store_before(TILES - 1)
            store_before(TILES)

        @block.gpsimd
        def _(pool):
            tile_no, late_no, down_no, up_no = (pool.alloc_register(n) for n in ("tile_no", "late_no", "down_no", "up_no"))
            for reg in (tile_no, late_no, down_no, up_no):
                pool.reg_mov(reg, DIAGS - RING if reg is up_no else 0)

            def wait_next(sem_, reg):
                pool.reg_add(reg, reg, 1)
                pool.wait_ge(consts_in, 48)
                pool.wait_ge(sem_, reg)

            def gather(ring, index, table, arrived, k):
                pool.indirect_dma_start(
                    out=ring[:, k % RING, :], out_offset=None, in_=table,
                    in_offset=bass.IndirectOffsetOnAxis(ap=index[:, k:k + 1], axis=0),
                ).then_inc(arrived[k % RING], 16)

            def down(k):
                if k == 0:
                    wait_next(handed, tile_no)
                wait_next(down_free, down_no)
                gather(down_ring, idxc, experts_down, down_in, k)

            def tile(last):
                for k in range(SLOTS):
                    if k + DOT_LEAD < SLOTS or not last:
                        down((k + DOT_LEAD) % SLOTS)
                    if k == HALF:
                        wait_next(handed_late, late_no)
                    wait_next(up_free, up_no)
                    gather(up_ring, idxu, experts_up, up_in, k)

            for k in range(DOT_LEAD):
                down(k)
            with pool.Fori(0, TILES - 1):
                tile(False)
            tile(True)

        @block.tensor
        def _(pe):
            pe.wait_ge(consts_in, 48)
            pe.sem_inc(up_free, DIAGS)

            def chunk(t, c, dst, src):
                pe.wait_ge(w_in[c % NW], t * PER_W + 16 * (c // NW + 1))
                n = chunk_cols(c)
                wc = wring[:, c % NW, 0:KT * n].rearrange("p (k n) -> p k n", k=KT)
                for k in range(KT):
                    last = pe.matmul(dst[:, 0:n], src[:, k, :], wc[:, k, :], start=k == 0, stop=k == KT - 1)
                last.then_inc(MM.sem, 1)

            def transposes(dst, blocks):
                for j, b in enumerate(blocks):
                    last = pe.transpose(dst[:, j, :], b, ident)
                return last

            def norm1_seg(t):
                if not isinstance(t, int):
                    pe.wait_ge(idx_ready, t)
                pe.wait_ge(N1.sem, N1.upto(t, 4))
                transposes(bank(0), [h[:, P * j:P * j + P] for j in range(4)])
                transposes(bank(1), [h[:, P * j:P * j + P] for j in range(4, 8)]).then_inc(N1.sem, 1)

            def project(c):
                def seg(t):
                    if c == 0:
                        pe.wait_ge(N1.sem, N1.upto(t, 6))
                    if c >= 4:
                        pe.wait_ge(EV.sem, EV.upto(t, c - 3))
                    chunk(t, c, W[:, 2 + c % 4, :], hT)
                return seg

            def transpose_seg(t):
                pe.wait_ge(EV.sem, EV.upto(t, N_IN))
                for g in range(3):
                    last = transposes(bank(2 + g), [proj[:, DN0 + P * b:DN0 + P * b + P]
                                                    for b in range(4 * g, 4 * g + 4)])
                last.then_inc(DN.sem, 1)
                pe.wait_ge(AT.sem, AT.upto(t, 8))
                transposes(bank(0), [flat(qk2[:, 2 * j:2 * j + 2, :]) for j in range(4)])
                pe.transpose(W[:, 1, 0:P], flat(qk2[:, AH:AH + KVH, :]), ident).then_inc(AT.sem, 1)

            def scores_seg(t):
                pe.wait_ge(AT.sem, AT.upto(t, 11))
                pe.wait_ge(DN.sem, DN.upto(t, 3))
                for j in range(4):
                    for a in range(2):
                        rows_ = slice(HD * a, HD * a + HD)
                        last = pe.matmul(W[:, 2 + 2 * a + j // 2, 256 * (j % 2):256 * (j % 2) + 256],
                                         qT[rows_, j, :], kTw[rows_, :], start=True, stop=True)
                last.then_inc(AT.sem, 1)

            def pv_seg(t):
                pe.wait_ge(AT.sem, AT.upto(t, 17))
                pr = bufA[:, :].rearrange("p (b n i) -> p b n i", b=4, n=4)
                for b in range(4):
                    last = transposes(bank(2 + b), [pr[:, b, n, :] for n in range(4)])
                last.then_inc(PT.sem, 1)
                pe.wait_ge(PT.sem, PT.upto(t, 3))
                pt = bufB[:, :].rearrange("p (h c i) -> p h c i", h=AH, c=2)
                for hh in range(AH):
                    kv = hh // (AH // KVH)
                    for c in range(2):
                        last = pe.matmul(W[:, 0, HD * hh:HD * hh + HD], pt[:, hh, c, :],
                                         v2[:, c, HD * kv:HD * kv + HD], start=c == 0, stop=c == 1)
                last.then_inc(PT.sem, 1)

            def qk_norm_seg(t):
                pe.wait_ge(DN.sem, DN.upto(t, 11))
                for g in range(2):
                    last = pe.matmul(W[:, 2 + g, :], ones, flat(yb[:, 4 * g:4 * g + 4, :]), start=True, stop=True)
                last.then_inc(DN.sem, 1)
                pe.wait_ge(DN.sem, DN.upto(t, 15))
                transposes(bank(4), [ya[:, 4 + b, :] for b in range(4)])
                transposes(bank(5), [ya[:, 8 + b, :] for b in range(4)]).then_inc(DN.sem, 1)

            def decay_seg(t):
                pe.wait_ge(PT.sem, PT.upto(t, 5))
                pe.wait_ge(GT.sem, GT.upto(t, 14))
                pe.matmul(W[:, 0, 0:DH], tri, gs[:, 13, :], start=True, stop=True).then_inc(GT.sem, 1)
                pe.wait_ge(GT.sem, GT.upto(t, 17))
                pe.matmul(W[:, 0, :], ones, flat(dg), start=True, stop=True)
                pe.matmul(W[:, 1, :], ones, flat(db), start=True, stop=True).then_inc(GT.sem, 1)

            def core_a(t):
                for hh in range(DH):
                    pe.matmul(bank(2)[:, hh, :], ya[:, 4 + hh, :], ya[:, 4 + hh, :], start=True, stop=True)
                for hh in range(DH):
                    last = pe.matmul(bank(3)[:, hh, :], ya[:, 4 + hh, :], ya[:, hh, :], start=True, stop=True)
                last.then_inc(CO.sem, 1)
                pe.wait_ge(DN.sem, DN.upto(t, 16))
                pe.wait_ge(SG.sem, SG.upto(t, 1))
                pe.wait_ge(GT.sem, GT.upto(t, 20))
                if isinstance(t, int):
                    pe.wait_ge(cleared, 4)
                for hh in range(DH):
                    pe.matmul(bank(5)[:, hh, :], ya[:, 4 + hh, :], state[:, hh, :], start=True, stop=True)
                for hh in range(DH):
                    last = pe.matmul(bank(0)[:, hh, :], ya[:, hh, :], state[:, hh, :], start=True, stop=True)
                last.then_inc(CO.sem, 1)

            def level(m):
                def seg(t):
                    pe.wait_ge(LM.sem, LM.upto(t, m + 1))
                    if m:
                        pe.wait_ge(LV.sem, LV.upto(t, 4 * m))
                    else:
                        pe.wait_ge(CO.sem, CO.upto(t, 4))
                    for hh in range(DH):
                        last = pe.matmul(bank(2)[:, hh, :], lm[:, m % 2, hh, :], inv[:, hh, :], start=True, stop=True)
                    last.then_inc(LV.sem, 1)
                    pe.wait_ge(LV.sem, LV.upto(t, 4 * m + 2))
                    for hh in range(DH):
                        last = pe.matmul(bank(4)[:, hh, :], yy[:, hh, :], invT[:, hh, :], start=True, stop=True)
                    if m < LEVELS - 1:
                        for hh in range(DH):
                            last = pe.matmul(bank(3)[:, hh, :], invT[:, hh, :], yy[:, hh, :], start=True, stop=True)
                    last.then_inc(LV.sem, 1)
                return seg

            def core_b(t):
                pe.wait_ge(LV.sem, LV.upto(t, 4 * LEVELS))
                for hh in range(DH):
                    last = pe.matmul(bank(2)[:, hh, :], invT[:, hh, :], rr[:, hh, :], start=True, stop=True)
                last.then_inc(CO.sem, 1)
                pe.wait_ge(CO.sem, CO.upto(t, 8))
                for hh in range(DH):
                    pe.matmul(bank(3)[:, hh, :], intra[:, hh, :], vn[:, hh, :], start=True, stop=True)
                for hh in range(DH):
                    last = pe.matmul(bank(4)[:, hh, :], kd[:, hh, :], vn[:, hh, :], start=True, stop=True)
                last.then_inc(CO.sem, 1)

            def mix_seg(t):
                pe.wait_ge(CO.sem, CO.upto(t, 18))
                transposes(bank(0), [mix[:, P * j:P * j + P] for j in range(4)])
                transposes(bank(1), [mix[:, P * j:P * j + P] for j in range(4, 8)]).then_inc(OU.sem, 1)

            def project_out(c):
                def seg(t):
                    pe.wait_ge(OU.sem, OU.upto(t, 2))
                    chunk(t, N_IN + c, W[:, 2 + c, :], hT)
                return seg

            def norm2_seg(t):
                pe.wait_ge(OU.sem, OU.upto(t, 7))
                transposes(bank(0), [h2[:, P * j:P * j + P] for j in range(4)])
                transposes(bank(1), [h2[:, P * j:P * j + P] for j in range(4, 8)]).then_inc(OU.sem, 1)

            def query(c):
                def seg(t):
                    if c < N_QRY:
                        pe.wait_ge(OU.sem, OU.upto(t, 9))
                        chunk(t, N_IN + N_OUT + c, W[:, 2 + c, :], hT)
                    if c > 0:
                        keys(t, c - 1)
                return seg

            def keys(t, c):
                pe.wait_ge(EV.sem, EV.upto(t, N_IN + c + 1))
                if c >= 2:
                    pe.wait_ge(QT.sem, QT.upto(t, 2 * c - 2))
                transposes(bank(c % 2), [bufA[:, CH * c + P * j:CH * c + P * j + P]
                                         for j in range(4)]).then_inc(QT.sem, 1)
                pe.wait_ge(QT.sem, QT.upto(t, 2 * c + 2))
                for j in range(4):
                    last = pe.matmul(W[:, 2 + c, P * j:P * j + P], bufB[:, CH * c + P * j:CH * c + P * j + P],
                                     keysT[:, j % 2, :], start=True, stop=True)
                last.then_inc(SC.sem, 1)

            def none(t):
                pass

            segments = [none, norm1_seg] + [project(c) for c in range(N_IN)] + [
                transpose_seg, scores_seg, pv_seg, qk_norm_seg, decay_seg, core_a] + [
                level(m) for m in range(LEVELS)] + [core_b, mix_seg, project_out(0), project_out(1), norm2_seg] + [
                query(c) for c in range(N_QRY + 1)] + [none, none, none]

            def slots(u, k0, k1):
                if k0 == k1:
                    return
                if k0 == 0:
                    pe.wait_ge(handed_late, u + 1)
                for k in range(k0, k1):
                    pe.wait_ge(diag_done, u * SLOTS + k + 1)
                    pe.wait_ge(up_in[k % RING], u * PER_RING + 16 * (k // RING + 1))
                    for c in range(2):
                        last = pe.matmul(acc[:, c, :], diag[:, k % DIAGS, :],
                                         up_ring[:, k % RING, CH * c:CH * c + CH],
                                         start=k == 0, stop=k == SLOTS - 1)
                    last.then_inc(up_free, 1)

            interleaved(pe, segments, slots)

        @block.scalar
        def _(act):
            act.wait_ge(consts_in, 48)
            act.activation(gs[:, 23, :], row[:, R_AL:R_AL + DH], ACT.Exp).then_inc(negA.sem, 1)

            def norm1_seg(t):
                if not isinstance(t, int):
                    act.wait_ge(idx_ready, t)
                act.wait_ge(x_in, t * 16 + 16)
                act.activation(h, xt[:, 0:D], ACT.Square, accum_out=st[:, 0:1]).then_inc(N1.sem, 1)
                act.wait_ge(N1.sem, N1.upto(t, 1))
                act.activation(st[:, 1:2], st[:, 0:1], ACT.Sqrt, bias=eps, scale=1.0 / D).then_inc(N1.sem, 1)
                act.wait_ge(N1.sem, N1.upto(t, 3))
                act.activation(h, xt[:, 0:D], ACT.Copy, scale=st[:, 2:3]).then_inc(N1.sem, 1)

            def copy_chunk(t, c, dst, src):
                act.wait_ge(MM.sem, MM.upto(t, c + 1))
                act.copy(dst, src).then_inc(EV.sem, 1)

            def project(c):
                def seg(t):
                    if c == 2:
                        act.wait_ge(EV.sem, EV.upto(t, 2))
                        act.activation(h[:, 0:QK_W], proj[:, 0:QK_W], ACT.Square).then_inc(AT.sem, 1)
                    if c == 3:
                        act.wait_ge(AT.sem, AT.upto(t, 2))
                        act.activation(st[:, 20:30], st[:, 10:20], ACT.Sqrt, bias=eps,
                                       scale=1.0 / HD).then_inc(AT.sem, 1)
                    n = chunk_cols(c)
                    copy_chunk(t, c, proj[:, CH * c:CH * c + n], W[:, 2 + c % 4, 0:n])
                return seg

            def transpose_seg(t):
                act.wait_ge(DN.sem, DN.upto(t, 2))
                for g in range(3):
                    last = act.copy(cin[:, 4 * g:4 * g + 4, CONV - 1:], bank(2 + g))
                last.then_inc(DN.sem, 1)
                act.wait_ge(AT.sem, AT.upto(t, 9))
                act.copy(qT[:, :, :], bank(0)).then_inc(AT.sem, 1)

            def scores_seg(t):
                act.wait_ge(AT.sem, AT.upto(t, 16))
                for hh in range(AH):
                    act.activation(bufA[:, 256 * hh:256 * hh + 256], bufA[:, 256 * hh:256 * hh + 256], ACT.Exp,
                                   bias=st[:, 40 + hh:41 + hh], accum_out=st[:, 56 + hh:57 + hh])
                act.activation(st[:, 64:72], st[:, 48:56], ACT.Exp).then_inc(AT.sem, 1)

            def pv_seg(t):
                act.wait_ge(PT.sem, PT.upto(t, 1))
                for b in range(2):
                    last = act.copy(bufB[:, CH * b:CH * b + CH], W[:, 2 + b, :])
                last.then_inc(PT.sem, 1)

            def qk_norm_seg(t):
                act.wait_ge(DN.sem, DN.upto(t, 9))
                act.activation(ya[:, :, :], ya[:, :, :], ACT.Silu).then_inc(DN.sem, 1)
                act.wait_ge(DN.sem, DN.upto(t, 10))
                act.activation(yb[:, 0:8, :], ya[:, 0:8, :], ACT.Square).then_inc(DN.sem, 1)
                act.wait_ge(DN.sem, DN.upto(t, 12))
                act.activation(yb[:, 0:8, :], W[:, 2:4, :].rearrange("p b (n i) -> p (b n) i", n=4), ACT.Sqrt,
                               bias=eps).then_inc(DN.sem, 1)
                act.activation(proj[:, GATE0:BETA0], proj[:, GATE0:BETA0], ACT.Silu)
                act.wait_ge(DN.sem, DN.upto(t, 16))
                act.copy(ktok, bank(4))
                act.copy(vtok, bank(5)).then_inc(SG.sem, 1)

            def decay_seg(t):
                act.wait_ge(GT.sem, GT.upto(t, 3))
                act.activation(gs[:, 3, :], gs[:, 2, :], ACT.Exp)
                act.activation(gs[:, 4, :], proj[:, BETA0:BETA0 + DH], ACT.Exp, scale=-1.0).then_inc(GT.sem, 1)
                act.wait_ge(GT.sem, GT.upto(t, 6))
                act.activation(gs[:, 8, :], gs[:, 5, :], ACT.Ln).then_inc(GT.sem, 1)
                act.wait_ge(GT.sem, GT.upto(t, 20))
                act.activation(dec, dec, ACT.Exp)
                act.activation(gs[:, 17:20, :], gs[:, 14:17, :], ACT.Exp).then_inc(GT.sem, 1)

            def none(t):
                pass

            def level(m):
                def seg(t):
                    act.wait_ge(LV.sem, LV.upto(t, 4 * m + 1))
                    act.copy(yy[:, :, :], bank(2)).then_inc(LV.sem, 1)
                return seg

            def core_b(t):
                act.wait_ge(CO.sem, CO.upto(t, 7))
                act.copy(vn[:, :, :], bank(2)).then_inc(CO.sem, 1)
                act.wait_ge(CO.sem, CO.upto(t, 11))
                act.activation(o_sq, o_dn, ACT.Square).then_inc(CO.sem, 1)
                act.wait_ge(CO.sem, CO.upto(t, 13))
                act.activation(gs[:, 21, :], gs[:, 20, :], ACT.Sqrt, bias=eps, scale=1.0 / DK).then_inc(CO.sem, 1)

            def mix_seg(t):
                act.wait_ge(OU.sem, OU.upto(t, 1))
                for g in range(2):
                    last = act.copy(hT[:, 4 * g:4 * g + 4, :], bank(g))
                last.then_inc(OU.sem, 1)

            def norm2_seg(t):
                act.wait_ge(OU.sem, OU.upto(t, 3))
                act.activation(h, x2[:, :], ACT.Square, accum_out=st[:, 80:81]).then_inc(OU.sem, 1)
                act.wait_ge(OU.sem, OU.upto(t, 4))
                act.activation(st[:, 81:82], st[:, 80:81], ACT.Sqrt, bias=eps, scale=1.0 / D).then_inc(OU.sem, 1)
                act.wait_ge(OU.sem, OU.upto(t, 8))
                for g in range(2):
                    last = act.copy(hT[:, 4 * g:4 * g + 4, :], bank(g))
                last.then_inc(OU.sem, 1)

            def query(c):
                def seg(t):
                    if c < N_QRY:
                        copy_chunk(t, N_IN + N_OUT + c, bufA[:, CH * c:CH * c + CH], W[:, 2 + c, :])
                    if c > 0:
                        act.wait_ge(QT.sem, QT.upto(t, 2 * c - 1))
                        act.copy(bufB[:, CH * c - CH:CH * c], W[:, (c - 1) % 2, :]).then_inc(QT.sem, 1)
                return seg

            def gate_exp(t):
                act.wait_ge(SM.sem, SM.upto(t, 1))
                act.activation(gates[:, :, :], gates[:, :, :], ACT.Exp).then_inc(SM.sem, 1)

            segments = [none, norm1_seg] + [project(c) for c in range(N_IN)] + [
                transpose_seg, scores_seg, pv_seg, qk_norm_seg, decay_seg, none] + [
                level(m) for m in range(LEVELS)] + [core_b, mix_seg, none, none, norm2_seg] + [
                query(c) for c in range(N_QRY + 1)] + [none, gate_exp, none]

            def slots(u, k0, k1):
                for k in range(k0, k1, 2):
                    act.wait_ge(down_free, u * SLOTS + RING + k + 2)
                    act.activation(act_s[:, k:k + 2], dots[:, k:k + 2], ACT.Gelu).then_inc(gelu_done, 1)
                    act.wait_ge(gelu_done, u * (SLOTS // 2) + k // 2 + 1)
                    for j in (k, k + 1):
                        act.activation(wgt[:, j:j + 1], act_s[:, j:j + 1], ACT.Copy,
                                       scale=gatesc[:, j:j + 1]).then_inc(wgt_done, 1)
                    act.wait_ge(wgt_done, u * SLOTS + k + 2)
                    for j in (k, k + 1):
                        act.wait_ge(up_free, u * SLOTS + j + 1)
                        act.activation(diag[:, j % DIAGS, :], ident, ACT.Copy,
                                       scale=wgt[:, j:j + 1]).then_inc(diag_done, 1)

            interleaved(act, segments, slots, DIAG_LEAD)

        @block.vector
        def _(dve):
            level_reg = dve.alloc_register("level_reg")

            def wait_before_max(stage, t, k):
                if isinstance(t, int):
                    dve.wait_ge(stage.sem, stage.upto(t, k))
                    return
                dve.reg_mul(level_reg, t, stage.n)
                dve.reg_add(level_reg, level_reg, k)
                dve.wait_ge(consts_in, 48)
                dve.wait_ge(stage.sem, level_reg)

            dve.memset(kTw[:, :], 0.0).then_inc(cleared, 1)
            dve.memset(v2[:, :, :], 0.0).then_inc(cleared, 1)
            dve.memset(cin[:, :, :], 0.0).then_inc(cleared, 1)
            dve.memset(state[:, :, :], 0.0).then_inc(cleared, 1)
            dve.wait_ge(consts_in, 48)
            dve.wait_ge(negA.sem, 1)
            dve.tensor_scalar(gs[:, 22, :], gs[:, 23, :], -1.0, None, ALU.mult).then_inc(negA.sem, 1)
            dve.wait_ge(negA.sem, 2)
            dve.wait_ge(cleared, 4)

            def norm1_seg(t):
                dve.wait_ge(N1.sem, N1.upto(t, 2))
                dve.reciprocal(st[:, 2:3], st[:, 1:2]).then_inc(N1.sem, 1)
                dve.wait_ge(N1.sem, N1.upto(t, 5))
                for g in range(2):
                    last = dve.tensor_tensor(hT[:, 4 * g:4 * g + 4, :], bank(g),
                                             over_last(norm1[:, 4 * g:4 * g + 4], P), ALU.mult)
                last.then_inc(N1.sem, 1)

            def none(t):
                pass

            def qk_seg(t):
                dve.wait_ge(AT.sem, AT.upto(t, 1))
                dve.tensor_reduce(st[:, 10:20], h[:, 0:QK_W].rearrange("p (n d) -> p n d", d=HD), AX.X,
                                  ALU.add).then_inc(AT.sem, 1)
                dve.wait_ge(AT.sem, AT.upto(t, 3))
                dve.reciprocal(st[:, 30:40], st[:, 20:30]).then_inc(AT.sem, 1)
                dve.wait_ge(AT.sem, AT.upto(t, 4))
                qk3 = qk.rearrange("p (n d) -> p n d", d=HD)
                dve.tensor_tensor(qk3, proj[:, 0:QK_W].rearrange("p (n d) -> p n d", d=HD),
                                  over_last(st[:, 30:40], HD), ALU.mult).then_inc(AT.sem, 1)
                dve.wait_ge(AT.sem, AT.upto(t, 5))
                for a in range(2):
                    dve.tensor_tensor(qk2[:, 0:AH, :].rearrange("p (j a) d -> p a j d", a=2)[:, a],
                                      qk3[:, 4 * a:4 * a + 4, :],
                                      row[:, R_QK:R_QK + 256].rearrange("p (n d) -> p n d", d=HD), ALU.mult)
                dve.tensor_tensor(qk2[:, AH:, :], qk3[:, AH:, :],
                                  row[:, R_QK + 512:R_QK + QK_W].rearrange("p (n d) -> p n d", d=HD),
                                  ALU.mult).then_inc(AT.sem, 1)
                dve.wait_ge(AT.sem, AT.upto(t, 6))
                x12 = qk2[:, :, 0:ROPE].rearrange("p n (s e) -> p n s e", s=2)
                for dst, c0 in ((rope_c, D), (rope_s, D + 8)):
                    for s in range(2):
                        last = dve.tensor_tensor(dst[:, :, s, :], x12[:, :, s, :],
                                                 over_mid(xt[:, c0:c0 + 8], AH + KVH), ALU.mult)
                last.then_inc(AT.sem, 1)
                dve.wait_ge(AT.sem, AT.upto(t, 7))
                dve.tensor_tensor(x12[:, :, 0, :], rope_c[:, :, 0, :], rope_s[:, :, 1, :], ALU.subtract)
                dve.tensor_tensor(x12[:, :, 1, :], rope_c[:, :, 1, :], rope_s[:, :, 0, :],
                                  ALU.add).then_inc(AT.sem, 1)

            def transpose_seg(t):
                dve.wait_ge(EV.sem, EV.upto(t, N_IN))
                dve.tensor_copy(v2[:, 0, :], v2[:, 1, :])
                dve.tensor_copy(kTw[:, 0:P], kTw[:, P:2 * P]).then_inc(MV.sem, 1)
                dve.tensor_copy(cin[:, :, 0:CONV - 1], cin[:, :, P:P + CONV - 1]).then_inc(DN.sem, 1)
                dve.wait_ge(MV.sem, MV.upto(t, 1))
                dve.tensor_copy(v2[:, 1, :], proj[:, QK_W:QK_W + P])
                dve.wait_ge(AT.sem, AT.upto(t, 9))
                dve.tensor_copy(kTw[:, P:2 * P], W[:, 1, 0:P]).then_inc(AT.sem, 1)

            def softmax_seg(t):
                c0 = C_M0 if isinstance(t, int) else C_M1
                s3 = bufA[:, :].rearrange("p (n k) -> p n k", n=AH)
                dve.wait_ge(AT.sem, AT.upto(t, 12))
                for b in range(4):
                    last = dve.scalar_tensor_tensor(
                        out=s3[:, 2 * b:2 * b + 2, :], in0=bank(2 + b, 2), scalar=HD ** -0.5,
                        in1=over_mid(cst[:, c0:c0 + 2 * P], 2), op0=ALU.mult, op1=ALU.add)
                last.then_inc(AT.sem, 1)
                dve.wait_ge(AT.sem, AT.upto(t, 13))
                dve.tensor_reduce(st[:, 72:80], s3, AX.X, ALU.max).then_inc(AT.sem, 1)
                dve.wait_ge(AT.sem, AT.upto(t, 14))
                dve.tensor_tensor(st[:, 72:80], st[:, 72:80], sinks, ALU.max).then_inc(AT.sem, 1)
                dve.wait_ge(AT.sem, AT.upto(t, 15))
                dve.tensor_scalar(st[:, 40:48], st[:, 72:80], -1.0, None, ALU.mult)
                dve.tensor_tensor(st[:, 48:56], sinks, st[:, 72:80], ALU.subtract).then_inc(AT.sem, 1)
                dve.wait_ge(AT.sem, AT.upto(t, 17))
                dve.tensor_tensor(st[:, 84:92], st[:, 56:64], st[:, 64:72], ALU.add).then_inc(AT.sem, 1)
                dve.wait_ge(AT.sem, AT.upto(t, 18))
                dve.reciprocal(st[:, 72:80], st[:, 84:92]).then_inc(AT.sem, 1)

            def conv_seg(t):
                dve.wait_ge(PT.sem, PT.upto(t, 1))
                for b in range(2, 4):
                    last = dve.tensor_copy(bufB[:, CH * b:CH * b + CH], W[:, 2 + b, :])
                last.then_inc(PT.sem, 1)

                def tap(dst, i):
                    return dve.tensor_tensor(dst[:, :, :], cin[:, :, i:i + P], over_last(convw[:, i, :], P), ALU.mult)

                dve.wait_ge(DN.sem, DN.upto(t, 3))
                tap(ya, 0)
                tap(yb, 1).then_inc(DN.sem, 1)
                for i in range(2, CONV + 1):
                    dve.wait_ge(DN.sem, DN.upto(t, 2 * i))
                    dve.tensor_tensor(ya[:, :, :], ya[:, :, :], yb[:, :, :], ALU.add).then_inc(DN.sem, 1)
                    if i < CONV:
                        dve.wait_ge(DN.sem, DN.upto(t, 2 * i + 1))
                        tap(yb, i).then_inc(DN.sem, 1)
                dve.wait_ge(AT.sem, AT.upto(t, 19))
                dve.wait_ge(PT.sem, PT.upto(t, 4))
                dve.tensor_tensor(mix[:, 0:512].rearrange("p (n d) -> p n d", d=HD), bank(0, AH),
                                  over_last(st[:, 72:80], HD), ALU.mult).then_inc(PT.sem, 1)

            def qk_norm_seg(t):
                dve.wait_ge(DN.sem, DN.upto(t, 13))
                dve.reciprocal(yb[:, 0:8, :], yb[:, 0:8, :]).then_inc(DN.sem, 1)
                dve.wait_ge(DN.sem, DN.upto(t, 14))
                dve.scalar_tensor_tensor(out=ya[:, 0:4, :], in0=yb[:, 0:4, :], scalar=DK ** -0.5, in1=ya[:, 0:4, :],
                                         op0=ALU.mult, op1=ALU.mult)
                dve.tensor_tensor(ya[:, 4:8, :], ya[:, 4:8, :], yb[:, 4:8, :], ALU.mult).then_inc(DN.sem, 1)

            def decay_seg(t):
                def g(n):
                    return gs[:, n, :]

                dve.tensor_tensor(g(0), proj[:, BETA0 + DH:IN_W], row[:, R_DT:R_DT + DH], ALU.add).then_inc(GT.sem, 1)
                dve.wait_ge(GT.sem, GT.upto(t, 1))
                dve.tensor_scalar(g(1), g(0), -1.0, None, ALU.mult).then_inc(GT.sem, 1)
                dve.wait_ge(GT.sem, GT.upto(t, 2))
                dve.tensor_tensor(g(2), g(0), g(1), ALU.min).then_inc(GT.sem, 1)
                dve.wait_ge(GT.sem, GT.upto(t, 4))
                dve.tensor_scalar(g(5), g(3), 1.0, None, ALU.add)
                dve.tensor_scalar(g(6), g(4), 1.0, None, ALU.add).then_inc(GT.sem, 1)
                dve.wait_ge(GT.sem, GT.upto(t, 5))
                dve.reciprocal(g(7), g(6)).then_inc(GT.sem, 1)
                dve.wait_ge(GT.sem, GT.upto(t, 7))
                dve.tensor_scalar(g(9), g(5), -1.0, None, ALU.add)
                dve.tensor_scalar(g(10), g(5), 1.0, None, ALU.is_equal).then_inc(GT.sem, 1)
                dve.wait_ge(GT.sem, GT.upto(t, 8))
                dve.tensor_tensor(g(9), g(9), g(10), ALU.add)
                dve.tensor_tensor(g(8), g(8), g(10), ALU.add).then_inc(GT.sem, 1)
                dve.wait_ge(GT.sem, GT.upto(t, 9))
                dve.reciprocal(g(11), g(9))
                dve.tensor_tensor(g(12), g(8), g(3), ALU.mult).then_inc(GT.sem, 1)
                dve.wait_ge(GT.sem, GT.upto(t, 10))
                dve.tensor_tensor(g(12), g(12), g(11), ALU.mult).then_inc(GT.sem, 1)
                dve.tensor_scalar(g(1), g(0), 0.0, None, ALU.max).then_inc(GT.sem, 1)
                dve.wait_ge(GT.sem, GT.upto(t, 12))
                dve.tensor_tensor(g(12), g(12), g(1), ALU.add).then_inc(GT.sem, 1)
                dve.wait_ge(GT.sem, GT.upto(t, 13))
                dve.tensor_tensor(g(13), g(12), g(22), ALU.mult).then_inc(GT.sem, 1)
                dve.wait_ge(GT.sem, GT.upto(t, 15))
                dve.tensor_copy(g(16), W[:, 0, 0:DH]).then_inc(GT.sem, 1)
                dve.wait_ge(GT.sem, GT.upto(t, 16))
                dve.tensor_tensor(dg, over_mid(ident, DH), over_last(g(16), P), ALU.mult)
                dve.tensor_tensor(db, over_mid(ident, DH), over_last(g(7), P), ALU.mult).then_inc(GT.sem, 1)
                dve.wait_ge(GT.sem, GT.upto(t, 18))
                for hh in range(DH):
                    dve.tensor_scalar(dec[:, hh, :], bank(0)[:, hh, :], gs[:, 16, hh:hh + 1], 0.0,
                                      ALU.subtract, ALU.min)
                dve.tensor_tensor(g(14), bank(0)[:, :, P - 1], g(16), ALU.subtract)
                dve.tensor_copy(g(15), bank(0)[:, :, P - 1]).then_inc(GT.sem, 1)
                dve.wait_ge(GT.sem, GT.upto(t, 19))
                dve.tensor_scalar(g(14), g(14), 0.0, None, ALU.min).then_inc(GT.sem, 1)
                dve.wait_ge(GT.sem, GT.upto(t, 21))
                dve.tensor_tensor(dec, dec, over_mid(tri, DH), ALU.mult)
                dve.tensor_tensor(gs[:, 20, :], g(7), g(19), ALU.mult)

            def masked(t, m):
                return dve.tensor_tensor(lm[:, m % 2], lt, over_mid(levels[:, m, :], DH), ALU.mult)

            def core_a(t):
                dve.wait_ge(CO.sem, CO.upto(t, 2))
                dve.tensor_copy(inv, over_mid(ident, DH))
                dve.tensor_copy(invT, over_mid(ident, DH)).then_inc(CO.sem, 1)
                dve.wait_ge(CO.sem, CO.upto(t, 3))
                dve.tensor_tensor(lt, bank(2), dec, ALU.mult).then_inc(CO.sem, 1)
                dve.tensor_tensor(intra, bank(3), dec, ALU.mult)
                dve.wait_ge(CO.sem, CO.upto(t, 4))
                dve.tensor_tensor(lt, lt, bank(1), ALU.mult).then_inc(CO.sem, 1)
                dve.wait_ge(SG.sem, SG.upto(t, 1))
                dve.tensor_tensor(ks_s, bank(5), over_last(gs[:, 20, :], P), ALU.mult)
                dve.tensor_tensor(vb, vtok, over_last(gs[:, 7, :], P), ALU.mult)
                dve.tensor_tensor(qs_s, bank(0), over_last(gs[:, 19, :], P), ALU.mult)
                dve.wait_ge(CO.sem, CO.upto(t, 5))
                masked(t, 0).then_inc(LM.sem, 1)
                dve.wait_ge(LM.sem, LM.upto(t, 1))
                dve.tensor_tensor(rr, vb, ks_s, ALU.subtract).then_inc(CO.sem, 1)
                dve.tensor_tensor(kd, ktok, over_last(gs[:, 17, :], P), ALU.mult)

            def level(m):
                def seg(t):
                    if m < LEVELS - 1:
                        masked(t, m + 1).then_inc(LM.sem, 1)
                    dve.wait_ge(LV.sem, LV.upto(t, 4 * m + 3))
                    if m < LEVELS - 1:
                        dve.tensor_tensor(inv, inv, bank(3), ALU.subtract)
                    dve.tensor_tensor(invT, invT, bank(4), ALU.subtract).then_inc(LV.sem, 1)
                return seg

            def core_b(t):
                dve.wait_ge(CO.sem, CO.upto(t, 9))
                dve.tensor_tensor(o_dn, qs_s, bank(3), ALU.add)
                dve.tensor_tensor(state[:, :, :], state[:, :, :], over_last(gs[:, 18, :], P),
                                  ALU.mult).then_inc(CO.sem, 1)
                dve.wait_ge(CO.sem, CO.upto(t, 10))
                dve.tensor_tensor(state[:, :, :], state[:, :, :], bank(4), ALU.add).then_inc(CO.sem, 1)
                dve.wait_ge(CO.sem, CO.upto(t, 12))
                dve.tensor_reduce(gs[:, 20, :], o_sq, AX.X, ALU.add).then_inc(CO.sem, 1)
                dve.wait_ge(CO.sem, CO.upto(t, 14))
                dve.reciprocal(gs[:, 20, :], gs[:, 21, :]).then_inc(CO.sem, 1)
                dve.wait_ge(CO.sem, CO.upto(t, 15))
                dve.tensor_tensor(o_dn, o_dn, over_last(gs[:, 20, :], P), ALU.mult).then_inc(CO.sem, 1)
                dve.wait_ge(CO.sem, CO.upto(t, 16))
                dve.tensor_tensor(o_dn, o_dn, over_mid(dn_w, DH), ALU.mult).then_inc(CO.sem, 1)
                dve.wait_ge(CO.sem, CO.upto(t, 17))
                dve.tensor_tensor(mix[:, 512:D], flat(o_dn), proj[:, GATE0:BETA0], ALU.mult).then_inc(CO.sem, 1)

            def out_seg(t):
                dve.wait_ge(MM.sem, MM.upto(t, N_IN + N_OUT))
                dve.tensor_tensor(x2[:, :], xt[:, 0:D], flat(W[:, 2:4, :]), ALU.add).then_inc(OU.sem, 1)

            def norm2_seg(t):
                dve.wait_ge(OU.sem, OU.upto(t, 5))
                dve.reciprocal(st[:, 82:83], st[:, 81:82]).then_inc(OU.sem, 1)
                dve.wait_ge(OU.sem, OU.upto(t, 6))
                dve.scalar_tensor_tensor(out=h2[:, :], in0=x2[:, :], scalar=st[:, 82:83], in1=norm2,
                                         op0=ALU.mult, op1=ALU.mult).then_inc(OU.sem, 1)

            s_in = flat(W[:, 2:6, :]).rearrange("p (n k) -> p n k", k=NKEY)

            def top(c):
                items, heads = range(4 * c, 4 * c + 4), range(2 * c, 2 * c + 2)
                sc2 = proj[:, 0:512].rearrange("p (n k) -> p n k", n=4)
                left = proj[:, 512:1024].rearrange("p (n k) -> p n k", n=2)
                own = proj[:, 1024:2048].rearrange("p (s m k) -> p s m k", s=2, k=TOPK)
                cand = bufA[:, CH * c:CH * c + CH].rearrange("p (n a b) -> p n a b", a=TOPK, b=TOPK)
                sums = bufA[:, CH * c:CH * c + CH].rearrange("p (n k) -> p n k", n=2)
                mine = slice(2 * TOPK * c, 2 * TOPK * c + 2 * TOPK)
                v_h = v16[:, 4 * c:4 * c + 4, :].rearrange("p (n s) k -> p n s k", s=2)
                i_h = i16f[:, 4 * c:4 * c + 4, :].rearrange("p (n s) k -> p n s k", s=2)

                def seg(t):
                    def after(k):
                        wait_before_max(TK, t, 15 * c + k)

                    wait_before_max(SC, t, c + 1)
                    for n in items:
                        last = dve.max(v16[:, n, 0:8], s_in[:, n, :])
                    last.then_inc(TK.sem, 1)
                    after(1)
                    for j, n in enumerate(items):
                        last = dve.match_replace(sc2[:, j, :], v16[:, n, 0:8], s_in[:, n, :], -3e38)
                    last.then_inc(TK.sem, 1)
                    after(2)
                    for j, n in enumerate(items):
                        last = dve.max(v16[:, n, 8:16], sc2[:, j, :])
                    last.then_inc(TK.sem, 1)
                    for n in items:
                        dve.max_index(i16[:, n, 0:8], v16[:, n, 0:8], s_in[:, n, :])
                    after(3)
                    for j, n in enumerate(items):
                        last = dve.max_index(i16[:, n, 8:16], v16[:, n, 8:16], sc2[:, j, :])
                    last.then_inc(TK.sem, 1)
                    for j in range(2):
                        last = dve.tensor_tensor(cand[:, j], over_last(v_h[:, j, 0, :], TOPK),
                                                 over_mid(v_h[:, j, 1, :], TOPK), ALU.add)
                    last.then_inc(TK.sem, 1)
                    after(5)
                    for j, n in enumerate(heads):
                        last = dve.max(top_s[:, n, 0:8], sums[:, j, :])
                    last.then_inc(TK.sem, 1)
                    after(6)
                    for j, n in enumerate(heads):
                        last = dve.match_replace(left[:, j, :], top_s[:, n, 0:8], sums[:, j, :], -3e38)
                    last.then_inc(TK.sem, 1)
                    after(7)
                    for j, n in enumerate(heads):
                        last = dve.max(top_s[:, n, 8:16], left[:, j, :])
                    last.then_inc(TK.sem, 1)
                    for j, n in enumerate(heads):
                        dve.max_index(sel[:, n, 0:8], top_s[:, n, 0:8], sums[:, j, :])
                    after(8)
                    for j, n in enumerate(heads):
                        last = dve.max_index(sel[:, n, 8:16], top_s[:, n, 8:16], left[:, j, :])
                    last.then_inc(TK.sem, 1)
                    dve.wait_ge(TK.sem, TK.upto(t, 15 * c + 9))
                    dve.tensor_scalar(sab[:, 0, mine], flat(sel[:, 2 * c:2 * c + 2, :]), 4, None,
                                      ALU.logical_shift_right)
                    dve.tensor_scalar(sab[:, 1, mine], flat(sel[:, 2 * c:2 * c + 2, :]), TOPK - 1, None,
                                      ALU.bitwise_and).then_inc(TK.sem, 1)
                    dve.wait_ge(TK.sem, TK.upto(t, 15 * c + 10))
                    dve.tensor_copy(sabf[:, :, mine], sab[:, :, mine])
                    dve.tensor_copy(i16f[:, 4 * c:4 * c + 4, :], i16[:, 4 * c:4 * c + 4, :]).then_inc(TK.sem, 1)
                    dve.wait_ge(TK.sem, TK.upto(t, 15 * c + 11))
                    for s_ in range(2):
                        last = dve.tensor_tensor(own[:, s_], over_last(sabf[:, s_, mine], TOPK),
                                                 over_mid(iota16, 2 * TOPK), ALU.is_equal)
                    last.then_inc(TK.sem, 1)
                    dve.wait_ge(TK.sem, TK.upto(t, 15 * c + 12))
                    for s_ in range(2):
                        for j in range(2):
                            part = own[:, s_, TOPK * j:TOPK * j + TOPK, :]
                            last = dve.tensor_tensor(part, part, over_mid(i_h[:, j, s_, :], TOPK), ALU.mult)
                    last.then_inc(TK.sem, 1)
                    dve.wait_ge(TK.sem, TK.upto(t, 15 * c + 13))
                    for s_ in range(2):
                        last = dve.tensor_reduce(pick[:, s_, mine], own[:, s_], AX.X, ALU.add)
                    last.then_inc(TK.sem, 1)
                    dve.wait_ge(TK.sem, TK.upto(t, 15 * c + 14))
                    dve.scalar_tensor_tensor(out=idx[:, mine], in0=pick[:, 0, mine], scalar=float(NKEY),
                                             in1=pick[:, 1, mine], op0=ALU.mult, op1=ALU.add).then_inc(TK.sem, 1)
                return seg

            def gate_seg(t):
                dve.tensor_tensor(gates[:, :, :], top_s[:, :, :], over_last(top_s[:, :, 0], TOPK),
                                  ALU.subtract).then_inc(SM.sem, 1)
                dve.wait_ge(SM.sem, SM.upto(t, 2))
                dve.tensor_reduce(gsum[:, 0, :], gates[:, :, :], AX.X, ALU.add).then_inc(SM.sem, 1)
                dve.wait_ge(SM.sem, SM.upto(t, 3))
                dve.reciprocal(gsum[:, 1, :], gsum[:, 0, :]).then_inc(SM.sem, 1)
                dve.wait_ge(SM.sem, SM.upto(t, 4))
                dve.tensor_tensor(gates[:, :, :], gates[:, :, :], over_last(gsum[:, 1, :], TOPK),
                                  ALU.mult).then_inc(idx_ready, 1)

            segments = [none, norm1_seg, none, none, none, qk_seg, none, none,
                        transpose_seg, softmax_seg, conv_seg, qk_norm_seg, decay_seg, core_a] + [
                level(m) for m in range(LEVELS)] + [core_b, none, none, out_seg, norm2_seg] + [
                none, none] + [top(c) for c in range(N_QRY)] + [gate_seg, none]

            def slots(u, k0, k1):
                for k in range(k0, k1):
                    dve.wait_ge(down_in[k % RING], u * PER_RING + 16 * (k // RING + 1))
                    down = down_ring[:, k % RING, :]
                    dve.tensor_tensor_reduce(out=down, in0=down, in1=h2c[:, :], scale=1.0, scalar=0.0,
                                             op0=ALU.mult, op1=ALU.add, accum_out=dots[:, k:k + 1]).then_inc(down_free, 1)

            def hand(t):
                if not isinstance(t, int):
                    dve.wait_ge(down_free, t * SLOTS + RING)
                    dve.wait_ge(wgt_done, t * SLOTS)
                dve.wait_ge(idx_ready, t + 1)
                dve.tensor_copy(idxc[:, :], idx[:, :])
                dve.tensor_copy(idxu[:, 0:HALF], idx[:, 0:HALF])
                dve.tensor_copy(gatesc[:, :], flat(gates[:, :, :]))
                dve.tensor_copy(h2c[:, :], h2[:, :]).then_inc(handed, 1)
                dve.wait_ge(handed, t + 1)

            def final(u, t):
                if u is not None:
                    dve.wait_ge(up_free, u * SLOTS + DIAGS + SLOTS)
                    if t is None:
                        dve.wait_ge(stored, 16 * u)
                    dve.tensor_tensor(out_sb[:, :], x2c[:, :], flat(acc[:, :, :]), ALU.add).then_inc(out_ready, 1)
                    dve.wait_ge(out_ready, u + 1)
                if t is not None:
                    dve.tensor_copy(idxu[:, HALF:SLOTS], idx[:, HALF:SLOTS])
                    dve.tensor_copy(x2c[:, :], x2[:, :]).then_inc(handed_late, 1)

            dve.sem_inc(down_free, RING)
            interleaved(dve, segments, slots, DOT_LEAD, hand, final)


def kernel(x, norm1_w, w_in, att_q_norm, att_k_norm, att_sinks, dn_conv_w, dn_A_log, dn_dt_bias, dn_out_norm,
           w_out, norm2_w, peer_w_query, peer_sub_keys1, peer_sub_keys2, peer_expert_down, peer_expert_up):
    import concourse.bacc as bacc
    from concourse.bass_utils import run_bass_kernel_spmd

    inv_freq = np.float32(500000.0) ** (-(np.arange(8, dtype=np.float32) * np.float32(2.0) / np.float32(ROPE)))
    ang = np.arange(SEQ, dtype=np.float32)[:, None] * inv_freq[None, :].astype(np.float32)
    i = np.arange(P)
    masks = [((i[None, :] // (2 * s) == i[:, None] // (2 * s)) & ((i[None, :] // s) % 2 == 1)
              & ((i[:, None] // s) % 2 == 0)) for s in (1 << m for m in range(LEVELS))]
    key = np.arange(2 * P)[None, :]
    valid = (key > i[:, None]) & (key <= i[:, None] + P)
    consts = np.concatenate(
        [np.eye(P), np.ones((P, P)), i[None, :] >= i[:, None]] + masks
        + [np.where(valid & (key >= P), 0.0, NEG), np.where(valid, 0.0, NEG),
           np.tile(np.arange(TOPK), (P, 1)), np.full((P, 1), EPS)], axis=1).astype(np.float32)

    def chunks(w):
        out_ = np.zeros((-(-w.shape[1] // CH), P, KT * CH), np.float32)
        for c in range(out_.shape[0]):
            part = w[:, c * CH:(c + 1) * CH]
            n = part.shape[1]
            out_[c, :, :KT * n] = part.reshape(KT, P, n).transpose(1, 0, 2).reshape(P, KT * n)
        return out_

    arrays = {
        "x_rope": np.concatenate([x[0], np.cos(ang), np.sin(ang)], axis=1),
        "weights": np.concatenate([chunks(w_in[0]), chunks(w_out[0]), chunks(peer_w_query[0])]),
        "experts_down": peer_expert_down[0],
        "experts_up": peer_expert_up[0],
        "rows": np.concatenate([np.tile(att_q_norm[0], AH), np.tile(att_k_norm[0], KVH), dn_dt_bias[0], dn_A_log[0],
                                att_sinks[0], dn_out_norm[0], norm2_w[0]])[None, :],
        "cols": np.concatenate([norm1_w[0].reshape(KT, P).T,
                                dn_conv_w[0].reshape(CONV, 12, P).transpose(2, 0, 1).reshape(P, CONV * 12),
                                peer_sub_keys1[0].T, peer_sub_keys2[0].T], axis=1),
        "consts": consts,
    }
    nc = bacc.Bacc("TRN2", target_bir_lowering=False, num_devices=1)
    arrays = {n: np.ascontiguousarray(a) for n, a in arrays.items()}
    aps = [nc.dram_tensor(n, a.shape, mybir.dt.from_np(a.dtype), kind="ExternalInput").ap()
           for n, a in arrays.items()]
    out = nc.dram_tensor("out", (SEQ, D), F32, kind="ExternalOutput").ap()
    build(nc, *aps, out)
    r = run_bass_kernel_spmd(nc, [arrays], core_ids=[0])
    return r.results[0]["out"].reshape(1, SEQ, D)
```

```python
from contextlib import ExitStack

import numpy as np
import concourse.bass as bass
from concourse import mybir

F32 = mybir.dt.float32
U32 = mybir.dt.uint32
ALU = mybir.AluOpType
ACT = mybir.ActivationFunctionType
AX = mybir.AxisListType

P = 128
SEQ, D = 1024, 1024
TILES, KT = SEQ // P, D // P
AH, KVH, HD, ROPE = 8, 2, 64, 16
DH, DK, CONV = 4, 128, 4
QK_W = (AH + KVH) * HD
DN0 = QK_W + KVH * HD
GATE0 = DN0 + 3 * DH * DK
BETA0 = GATE0 + DH * DK
IN_W = BETA0 + 2 * DH
CH = 512
N_IN, N_OUT, N_QRY = -(-IN_W // CH), D // CH, 4
PH, NKEY, TOPK = 8, 128, 16
SLOTS = PH * TOPK
EPS = 1e-6
LEVELS = 7
RING = 8
DOT_LEAD = 8
DIAG_LEAD = 4
HALF = SLOTS // 2
NW = 2
DIAGS = 8
NEG = -1e30
R_QK, R_DT, R_AL, R_SINK, R_DNW, R_N2 = 0, QK_W, QK_W + DH, QK_W + 2 * DH, QK_W + 2 * DH + AH, QK_W + 2 * DH + AH + DK
R_W = R_N2 + D
C_ID, C_ONE, C_TRI, C_LEV = 0, P, 2 * P, 3 * P
C_M0 = C_LEV + LEVELS * P
C_M1 = C_M0 + 2 * P
C_IOTA = C_M1 + 2 * P
C_EPS = C_IOTA + TOPK
C_W = C_EPS + 1
K_N1, K_CONV, K_KEYS = 0, KT, KT + CONV * 12
K_W = K_KEYS + 2 * NKEY

FIRST, BOTH, LOADED = "first", "both", "loaded"
SEG_SLOTS = {
    BOTH: [4, 4, 2, 2] + [2, 2] * N_IN + [4, 4, 4, 4, 4, 4, 2, 4] + [2, 4] * 3 + [2] + [4, 0, 2, 2, 4]
    + [2, 4, 4, 4] + [4, 6, 4, 2],
    LOADED: [2, 4, 4] + [4, 4, 4, 4, 4, 4, 4, 4] + [4] * LEVELS + [4, 4, 4, 4, 4] + [4] * N_QRY + [4, 8, 6, 4],
}


class Place:

    def __init__(self, r, mul, add):
        self.r, self.mul, self.add = r, mul, add

    def times(self, n, k=0):
        if self.r is None:
            return self.add * n + k
        return self.r * (self.mul * n) + (self.add * n + k)

    def scaled(self, n, k):
        return Place(self.r, self.mul * n, self.add * n + k)

    def before(self):
        return Place(self.r, self.mul, self.add - 1)

    def after(self):
        return Place(self.r, self.mul, self.add + 1)


N_TAIL = N_OUT - 1 + N_QRY
START = 2 * N_IN + N_TAIL
PER_PAIR = N_TAIL + N_IN + N_TAIL


class Tile:

    def __init__(self, pair, kind):
        self.kind, self.first = kind, kind == FIRST
        if kind == FIRST:
            self.number = self.round = self.in_at = self.copied = Place(None, 0, 0)
            self.next_at, self.tail_at = Place(None, 0, N_IN), Place(None, 0, 2 * N_IN)
        elif kind == LOADED:
            self.number, self.round = pair.scaled(2, 1), pair
            self.tail_at = pair.scaled(PER_PAIR, START)
        else:
            self.number, self.round = pair.scaled(2, 2), pair.scaled(1, 1)
            self.in_at = pair.scaled(PER_PAIR, START + N_TAIL)
            self.tail_at = pair.scaled(PER_PAIR, START + N_TAIL + N_IN)
            self.copied = pair.scaled(2 * N_IN, 2 * N_IN)


class Steps:

    def __init__(self, sem, n):
        self.sem, self.n = sem, n

    def upto(self, t, k):
        return t.number.times(self.n, k)


class RoundSteps(Steps):

    def __init__(self, sem, n, first=0):
        self.sem, self.n, self.first = sem, n, first

    def upto(self, t, k):
        return t.round.times(self.n, k - self.first * self.n)


assert TILES % 2 == 0 and PER_PAIR % NW == 0
PAIRS = TILES // 2 - 1


def chunk_cols(c):
    return min(CH, IN_W - c * CH) if c < N_IN else CH


def build(nc, x_rope, weights, experts_down, experts_up, rows, cols, consts, spill, out):
    with ExitStack() as ctx:
        def sb(name, shape, dt=F32):
            return ctx.enter_context(nc.sbuf_tensor(name, shape, dt))

        def sem(name):
            return ctx.enter_context(nc.semaphore(name))

        def steps(name, n):
            return Steps(sem(name), n)

        down_ring = sb("down_ring", [P, RING, D])
        up_ring = sb("up_ring", [P, RING, D])
        wring = sb("wring", [P, NW, KT * CH])
        cst = sb("cst", [P, C_W])
        row = sb("row", [P, R_W])
        col = sb("col", [P, K_W])
        xt = sb("xt", [P, D + ROPE])
        resident = sb("resident", [P, KT * CH])
        proj = sb("proj", [P, IN_W])
        qT = sb("qT", [P, AH // 2, P])
        kTw = sb("kTw", [P, 2 * P])
        v2 = sb("v2", [P, 2, P])
        bufA = sb("bufA", [P, 2048])
        bufB = sb("bufB", [P, 2048])
        st = sb("st", [P, 96])
        gs = sb("gs", [P, 24, DH])
        cin = sb("cin", [P, 12, CONV - 1 + P])
        yab = sb("yab", [P, 24, P])
        state = sb("state", [P, DH, P])
        mix = sb("mix", [P, D])
        x2c = sb("x2c", [P, D])
        h2c = sb("h2c", [P, D])
        v16 = sb("v16", [P, 2 * PH, TOPK])
        i16 = sb("i16", [P, 2 * PH, TOPK], U32)
        top_s = sb("top_s", [P, PH, TOPK])
        sel = sb("sel", [P, PH, TOPK], U32)
        sab = sb("sab", [P, 2, SLOTS], U32)
        gates = sb("gates", [P, PH, TOPK])
        gsum = sb("gsum", [P, 2, PH])
        idx = sb("idx", [P, SLOTS], U32)
        idxc = sb("idxc", [P, SLOTS], U32)
        idxu = sb("idxu", [P, SLOTS], U32)
        gatesc = sb("gatesc", [P, SLOTS])
        dots = sb("dots", [P, SLOTS])
        act_s = sb("act_s", [P, SLOTS])
        wgt = sb("wgt", [P, SLOTS])
        diag = sb("diag", [P, DIAGS, P])
        W = ctx.enter_context(nc.psum_tensor("W", [P, 6, 512], F32))
        acc = ctx.enter_context(nc.psum_tensor("acc", [P, 2, 512], F32))

        ident, ones, tri = (cst[:, c:c + P] for c in (C_ID, C_ONE, C_TRI))
        levels = cst[:, C_LEV:C_LEV + LEVELS * P].rearrange("p (l i) -> p l i", l=LEVELS)
        iota16 = cst[:, C_IOTA:C_IOTA + TOPK]
        eps = cst[:, C_EPS:C_EPS + 1]
        norm1 = col[:, K_N1:K_N1 + KT]
        convw = col[:, K_CONV:K_CONV + CONV * 12].rearrange("p (i b) -> p i b", i=CONV)
        keysT = col[:, K_KEYS:K_KEYS + 2 * NKEY].rearrange("p (s k) -> p s k", s=2)
        sinks = row[:, R_SINK:R_SINK + AH]
        dn_w = row[:, R_DNW:R_DNW + DK]
        norm2 = row[:, R_N2:R_N2 + D]
        yb, ya = yab[:, 0:12, :], yab[:, 12:24, :]
        x2 = yab[:, 8:16, :].rearrange("p n i -> p (n i)")
        h = bufA[:, 0:D]
        bA = bufA[:, :].rearrange("p (n h i) -> p n h i", n=4, h=DH)
        bB = bufB[:, :].rearrange("p (n h i) -> p n h i", n=4, h=DH)
        dg, db, lt, yy = (bA[:, n] for n in range(4))
        inv, invT = bA[:, 0], bA[:, 1]
        ks_s, vtok, rr, vn = (bB[:, n] for n in range(4))
        vb = vtok
        hT = ya[:, 4:12, :]
        yflat = yb[:, :, :].rearrange("p n i -> p (n i)")
        qk = yflat[:, 0:QK_W]
        qk2 = yflat[:, QK_W:2 * QK_W].rearrange("p (n d) -> p n d", d=HD)
        h2 = yflat[:, 0:D]
        rope_c = yflat[:, 2 * QK_W:2 * QK_W + 160].rearrange("p (n s e) -> p n s e", s=2, e=8)
        rope_s = ya[:, 0:2, 0:80].rearrange("p s (n e) -> p n s e", e=8)
        qs_s, ktok, o_sq = yb[:, 0:4, :], yb[:, 4:8, :], yb[:, 8:12, :]
        kd = ktok
        o_dn = ya[:, 0:4, :]
        dec = proj[:, 0:512].rearrange("p (h i) -> p h i", h=DH)
        lm = proj[:, DN0:DN0 + 1024].rearrange("p (n h i) -> p n h i", n=2, h=DH)
        intra = proj[:, DN0 + 1024:DN0 + 1536].rearrange("p (h i) -> p h i", h=DH)
        sabf = mix[:, 0:256].rearrange("p (s m) -> p s m", s=2)
        pick = mix[:, 256:512].rearrange("p (s m) -> p s m", s=2)
        i16f = mix[:, 512:768].rearrange("p (n k) -> p n k", k=TOPK)
        out_sb = mix

        def bank(b, n=4):
            return W[:, b, :].rearrange("p (n i) -> p n i", n=n)

        def flat(ap):
            return ap.rearrange("p a b -> p (a b)")

        def over_last(ap, n):
            return ap.unsqueeze(2).broadcast_to([P, ap.shape[1], n])

        def over_mid(ap, n):
            return ap.unsqueeze(1).broadcast_to([P, n, ap.shape[1]])

        class NextTile:

            def __init__(self, first):
                self.own = (up_ring[:, 6, :] if first else yflat[:, 0:D]).rearrange("p (k n) -> p k n", k=KT)
                self.x = up_ring[:, 0, :] if first else bufB[:, 0:D]
                self.h = up_ring[:, 1, :] if first else bufA[:, D:2 * D]
                self.hT = up_ring[:, 2, :].rearrange("p (k n) -> p k n", k=KT) if first else ya[:, 4:12, :]
                late = up_ring[:, 5, :] if first else self.h
                self.parts = [flat(up_ring[:, 3:5, :]) if first else bufB[:, :], late[:, 0:IN_W - 4 * CH]]
                self.banks = [acc[:, 0, :], acc[:, 1, :]] if first else [W[:, 0, :], W[:, 1, :]]

            def staged(self, c):
                at = CH * (c % 4)
                return self.parts[c // 4][:, at:at + chunk_cols(c)]


        consts_in = sem("consts_in")
        x_in = sem("x_in")
        w_in = [sem(f"w_in{i}") for i in range(NW)]
        down_in = [sem(f"down_in{i}") for i in range(RING)]
        up_in = [sem(f"up_in{i}") for i in range(RING)]
        resident_in = sem("resident_in")
        negA = steps("neg_exp_a", 2)
        cleared = sem("cleared")
        xb_in = sem("xb_in")
        spilled = sem("spilled")
        proj_in = sem("proj_in")
        N1 = RoundSteps(sem("norm1_step"), 6)
        NB = RoundSteps(sem("norm1_next"), 6)
        chunk_used = sem("chunk_used")
        FP = RoundSteps(sem("first_product"), N_IN, 1)
        MV = steps("window_moved", 1)
        in_copied = sem("in_copied")
        QC = steps("query_copied", N_QRY)
        AT = steps("att_step", 19)
        PT = steps("probs_t", 5)
        DN = steps("dn_step", 16)
        GT = steps("gate_step", 21)
        SG = steps("silu_gate", 1)
        CO = steps("core_step", 18)
        LV = steps("level_step", 4 * LEVELS)
        LM = steps("level_mask", LEVELS)
        OU = steps("out_step", 9)
        QT = steps("query_t", 2 * N_QRY)
        SC = steps("key_scores", N_QRY)
        TK = steps("topk_step", 15 * N_QRY)
        SM = steps("gate_softmax", 4)
        idx_ready = sem("idx_ready")
        idx_first = sem("idx_first")
        handed = sem("handed")
        handed_late = sem("handed_late")
        down_free = sem("down_free")
        gelu_done = sem("gelu_done")
        wgt_done = sem("wgt_done")
        diag_done = sem("diag_done")
        up_free = sem("up_free")
        out_ready = sem("out_ready")
        stored = sem("stored")

        block = ctx.enter_context(nc.Block())
        PER_RING = 16 * SLOTS // RING

        def slot_and_count(at, c):
            return (at.add + c) % NW, Place(at.r, at.mul // NW, (at.add + c) // NW + 1).times(16)

        def is_first(t):
            return t.r is None and t.add == 0

        def wait_projected(eng, t):
            if t.kind == LOADED:
                eng.wait_ge(proj_in, t.round.times(16, 16))
            else:
                eng.wait_ge(in_copied, t.copied.times(1, 2 * N_IN if t.kind == BOTH else N_IN))

        def interleaved(eng, segments, slots, lead=0, hand=lambda t: None, final=lambda u, t: None):
            def body(t):
                u, k = t.number.before(), lead
                assert len(segments[t.kind]) == len(SEG_SLOTS[t.kind]) and sum(SEG_SLOTS[t.kind]) == SLOTS
                for seg, n in zip(segments[t.kind], SEG_SLOTS[t.kind]):
                    seg(t)
                    slots(u, min(k, SLOTS), min(k + n, SLOTS))
                    k += n
                hand(t.number)
                slots(t.number, 0, lead)
                final(u, t.number)

            t0, last = Tile(None, FIRST), Tile(Place(None, 0, PAIRS), LOADED)
            for seg in segments[FIRST]:
                seg(t0)
            hand(t0.number)
            slots(t0.number, 0, lead)
            final(None, t0.number)
            with eng.Fori(0, PAIRS) as r:
                pair = Place(r, 1, 0)
                body(Tile(pair, LOADED))
                body(Tile(pair, BOTH))
            body(last)
            slots(last.number, lead, SLOTS)
            final(last.number, None)

        @block.sync
        def _(sp):
            sp.dma_start(cst[:, :], consts).then_inc(consts_in, 16)
            sp.dma_start(row[:, :], rows.broadcast_to([P, R_W])).then_inc(consts_in, 16)
            sp.dma_start(col[:, :], cols).then_inc(consts_in, 16)

            counted = sp.alloc_register("counted")

            def wait_apart(sem_, place, n, k):
                if place.r is None:
                    sp.wait_ge(sem_, place.times(n, k))
                    return
                sp.reg_mul(counted, place.r, place.mul * n)
                sp.reg_add(counted, counted, place.add * n + k)
                sp.wait_ge(consts_in, 48)
                sp.wait_ge(sem_, counted)

            def tokens(place):
                return slice(place.add * P, place.add * P + P) if place.r is None else bass.ds(place.times(P), P)

            def load_chunks(at, first, chunks, wait=True):
                for c in chunks:
                    if wait:
                        sp.wait_ge(chunk_used, at.times(1, c - NW + 1))
                    n, slot = chunk_cols(first + c), slot_and_count(at, c)[0]
                    sp.dma_start(wring[:, slot, 0:KT * n], weights[first + c, :, 0:KT * n]).then_inc(w_in[slot], 16)

            def load_x(t):
                sp.dma_start(xt[:, :], x_rope[tokens(t.number), :]).then_inc(x_in, 16)

            def load_next_x(t):
                nxt = NextTile(t.first)
                sp.dma_start(nxt.x, x_rope[tokens(t.number.after()), 0:D]).then_inc(xb_in, 16)

            def spill_part(t, part, copies):
                sp.wait_ge(in_copied, t.copied.times(1, copies))
                cols_ = slice(0, 4 * CH) if part == 0 else slice(4 * CH, IN_W)
                sp.dma_start(spill[:, cols_], NextTile(t.first).parts[part]).then_inc(spilled, 16)

            def ahead(t):
                wait_apart(OU.sem, t.number.before(), OU.n, 3)
                load_x(t)
                if t.kind == LOADED:
                    load_chunks(t.tail_at, N_IN + 1, range(NW))
                    sp.wait_ge(spilled, t.round.times(32, 32))
                    sp.wait_ge(idx_ready, t.number.times(1))
                    sp.dma_start(proj[:, :], spill).then_inc(proj_in, 16)
                else:
                    load_chunks(t.in_at, 0, range(NW))
                    wait_apart(idx_ready, t.number, 1, 0)
                    load_next_x(t)

            def rest(t):
                if t.kind == BOTH:
                    load_chunks(t.in_at, 0, range(NW, N_IN))
                    spill_part(t, 0, 8)
                    load_chunks(t.tail_at, N_IN + 1, range(NW))
                    spill_part(t, 1, 2 * N_IN)
                load_chunks(t.tail_at, N_IN + 1, range(NW, N_TAIL))

            def store_before(place):
                u = place.before()
                wait_apart(out_ready, place, 1, 0)
                sp.dma_start(out[tokens(u), :], out_sb[:, :]).then_inc(stored, 16)
                wait_apart(stored, place, 16, 16)

            t0, last = Tile(None, FIRST), Tile(Place(None, 0, PAIRS), LOADED)
            sp.sem_inc(stored, 16)
            load_x(t0)
            load_chunks(t0.in_at, 0, range(NW), wait=False)
            load_next_x(t0)
            load_chunks(t0.in_at, 0, range(NW, N_IN))
            load_chunks(t0.next_at, 0, range(N_IN))
            sp.dma_start(resident[:, :], weights[N_IN, :, :]).then_inc(resident_in, 16)
            spill_part(t0, 0, N_IN + 4)
            load_chunks(t0.tail_at, N_IN + 1, range(NW))
            spill_part(t0, 1, 2 * N_IN)
            load_chunks(t0.tail_at, N_IN + 1, range(NW, N_TAIL))
            ahead(Tile(Place(None, 0, 0), LOADED))
            with sp.Fori(0, PAIRS) as r:
                pair = Place(r, 1, 0)
                t, t_next = Tile(pair, LOADED), Tile(pair, BOTH)
                rest(t)
                ahead(t_next)
                store_before(t.number)
                rest(t_next)
                ahead(Tile(pair.after(), LOADED))
                store_before(t_next.number)
            rest(last)
            store_before(last.number)
            store_before(last.number.after())

        @block.gpsimd
        def _(pool):
            tile_no, late_no, down_no, up_no = (pool.alloc_register(n) for n in ("tile_no", "late_no", "down_no", "up_no"))
            for reg in (tile_no, late_no, down_no, up_no):
                pool.reg_mov(reg, DIAGS - RING if reg is up_no else 0)

            def wait_next(sem_, reg):
                pool.reg_add(reg, reg, 1)
                pool.wait_ge(consts_in, 48)
                pool.wait_ge(sem_, reg)

            def gather(ring, index, table, arrived, k):
                pool.indirect_dma_start(
                    out=ring[:, k % RING, :], out_offset=None, in_=table,
                    in_offset=bass.IndirectOffsetOnAxis(ap=index[:, k:k + 1], axis=0),
                ).then_inc(arrived[k % RING], 16)

            def down(k, new=0):
                if k == new:
                    wait_next(handed, tile_no)
                wait_next(down_free, down_no)
                gather(down_ring, idxc, experts_down, down_in, k)

            def up(k):
                if k == HALF:
                    wait_next(handed_late, late_no)
                wait_next(up_free, up_no)
                gather(up_ring, idxu, experts_up, up_in, k)

            pool.wait_ge(idx_first, 1)
            for k in range(RING):
                down(k, new=RING)
            pool.wait_ge(spilled, 32)
            for k in range(RING):
                up(k)
            for k in range(RING, SLOTS):
                down(k, new=RING)
                if k >= RING + DOT_LEAD:
                    up(k - DOT_LEAD)
            for k in range(SLOTS - DOT_LEAD, SLOTS):
                up(k)
            with pool.Fori(1, TILES):
                for k in range(SLOTS + DOT_LEAD):
                    if k < SLOTS:
                        down(k)
                    if k >= DOT_LEAD:
                        up(k - DOT_LEAD)

        @block.tensor
        def _(pe):
            pe.wait_ge(consts_in, 48)
            pe.sem_inc(up_free, DIAGS)

            def product(dst, src, wc, n=CH):
                wc = wc[:, 0:KT * n].rearrange("p (k n) -> p k n", k=KT)
                for k in range(KT):
                    last = pe.matmul(dst[:, 0:n], src[:, k, :], wc[:, k, :], start=k == 0, stop=k == KT - 1)
                return last

            def chunk(at, c, dst, src, n=CH, done=chunk_used):
                slot, count = slot_and_count(at, c)
                pe.wait_ge(w_in[slot], count)
                product(dst, src, wring[:, slot, :], n).then_inc(done, 1)

            def transposes(dst, blocks):
                for j, b in enumerate(blocks):
                    last = pe.transpose(dst[:, j, :], b, ident)
                return last

            def norm1_seg(t):
                if not t.first:
                    pe.wait_ge(idx_ready, t.number.times(1))
                pe.wait_ge(N1.sem, N1.upto(t, 4))
                transposes(bank(0), [h[:, P * j:P * j + P] for j in range(4)])
                transposes(bank(1), [h[:, P * j:P * j + P] for j in range(4, 8)]).then_inc(N1.sem, 1)

            def norm1_next(t):
                nxt = NextTile(t.first)
                pe.wait_ge(NB.sem, NB.upto(t, 4))
                for g in range(2):
                    last = transposes(nxt.banks[g].rearrange("p (n i) -> p n i", n=4),
                                      [nxt.h[:, P * j:P * j + P] for j in range(4 * g, 4 * g + 4)])
                last.then_inc(NB.sem, 1)

            def project(c):
                def seg(t):
                    n = 2 * c if t.kind == BOTH else c
                    if c == 0:
                        pe.wait_ge(N1.sem, N1.upto(t, 6))
                    if n >= 4:
                        pe.wait_ge(in_copied, t.copied.times(1, n - 3))
                    chunk(t.in_at, c, W[:, 2 + n % 4, :], NextTile(t.first).own, chunk_cols(c),
                          FP.sem if t.kind == BOTH else chunk_used)
                return seg

            def project_next(c):
                def seg(t):
                    if c == 0:
                        pe.wait_ge(NB.sem, NB.upto(t, 6))
                    if t.first:
                        if c >= 2:
                            pe.wait_ge(in_copied, N_IN + c - 1)
                        chunk(t.next_at, c, acc[:, c % 2, :], NextTile(True).hT, chunk_cols(c))
                        return
                    n = 2 * c + 1
                    if n >= 4:
                        pe.wait_ge(in_copied, t.copied.times(1, n - 3))
                    chunk(t.in_at, c, W[:, 2 + n % 4, :], NextTile(False).hT, chunk_cols(c))
                return seg

            def transpose_seg(t):
                wait_projected(pe, t)
                for g in range(3):
                    last = transposes(bank(2 + g), [proj[:, DN0 + P * b:DN0 + P * b + P]
                                                    for b in range(4 * g, 4 * g + 4)])
                last.then_inc(DN.sem, 1)
                pe.wait_ge(AT.sem, AT.upto(t, 8))
                transposes(bank(0), [flat(qk2[:, 2 * j:2 * j + 2, :]) for j in range(4)])
                pe.transpose(W[:, 1, 0:P], flat(qk2[:, AH:AH + KVH, :]), ident).then_inc(AT.sem, 1)

            def scores_seg(t):
                pe.wait_ge(AT.sem, AT.upto(t, 11))
                pe.wait_ge(DN.sem, DN.upto(t, 3))
                for j in range(4):
                    for a in range(2):
                        rows_ = slice(HD * a, HD * a + HD)
                        last = pe.matmul(W[:, 2 + 2 * a + j // 2, 256 * (j % 2):256 * (j % 2) + 256],
                                         qT[rows_, j, :], kTw[rows_, :], start=True, stop=True)
                last.then_inc(AT.sem, 1)

            def pv_seg(t):
                pe.wait_ge(AT.sem, AT.upto(t, 17))
                pr = bufA[:, :].rearrange("p (b n i) -> p b n i", b=4, n=4)
                for b in range(4):
                    last = transposes(bank(2 + b), [pr[:, b, n, :] for n in range(4)])
                last.then_inc(PT.sem, 1)
                pe.wait_ge(PT.sem, PT.upto(t, 3))
                pt = bufB[:, :].rearrange("p (h c i) -> p h c i", h=AH, c=2)
                for hh in range(AH):
                    kv = hh // (AH // KVH)
                    for c in range(2):
                        last = pe.matmul(W[:, 0, HD * hh:HD * hh + HD], pt[:, hh, c, :],
                                         v2[:, c, HD * kv:HD * kv + HD], start=c == 0, stop=c == 1)
                last.then_inc(PT.sem, 1)

            def qk_sums(t):
                pe.wait_ge(DN.sem, DN.upto(t, 11))
                for g in range(2):
                    last = pe.matmul(W[:, 2 + g, :], ones, flat(yb[:, 4 * g:4 * g + 4, :]), start=True, stop=True)
                last.then_inc(DN.sem, 1)

            def kv_transposed(t):
                pe.wait_ge(DN.sem, DN.upto(t, 15))
                transposes(bank(4), [ya[:, 4 + b, :] for b in range(4)])
                transposes(bank(5), [ya[:, 8 + b, :] for b in range(4)]).then_inc(DN.sem, 1)

            def qk_norm_seg(t):
                qk_sums(t)
                kv_transposed(t)

            def decay_seg(t):
                pe.wait_ge(PT.sem, PT.upto(t, 5))
                pe.wait_ge(GT.sem, GT.upto(t, 14))
                pe.matmul(W[:, 0, 0:DH], tri, gs[:, 13, :], start=True, stop=True).then_inc(GT.sem, 1)
                pe.wait_ge(GT.sem, GT.upto(t, 17))
                pe.matmul(W[:, 0, :], ones, flat(dg), start=True, stop=True)
                pe.matmul(W[:, 1, :], ones, flat(db), start=True, stop=True).then_inc(GT.sem, 1)

            def core_a(t):
                for hh in range(DH):
                    pe.matmul(bank(2)[:, hh, :], ya[:, 4 + hh, :], ya[:, 4 + hh, :], start=True, stop=True)
                for hh in range(DH):
                    last = pe.matmul(bank(3)[:, hh, :], ya[:, 4 + hh, :], ya[:, hh, :], start=True, stop=True)
                last.then_inc(CO.sem, 1)
                pe.wait_ge(DN.sem, DN.upto(t, 16))
                pe.wait_ge(SG.sem, SG.upto(t, 1))
                pe.wait_ge(GT.sem, GT.upto(t, 20))
                if t.first:
                    pe.wait_ge(cleared, 4)
                for hh in range(DH):
                    pe.matmul(bank(5)[:, hh, :], ya[:, 4 + hh, :], state[:, hh, :], start=True, stop=True)
                for hh in range(DH):
                    last = pe.matmul(bank(0)[:, hh, :], ya[:, hh, :], state[:, hh, :], start=True, stop=True)
                last.then_inc(CO.sem, 1)

            def level(m):
                def seg(t):
                    pe.wait_ge(LM.sem, LM.upto(t, m + 1))
                    if m:
                        pe.wait_ge(LV.sem, LV.upto(t, 4 * m))
                    else:
                        pe.wait_ge(CO.sem, CO.upto(t, 4))
                    for hh in range(DH):
                        last = pe.matmul(bank(2)[:, hh, :], lm[:, m % 2, hh, :], inv[:, hh, :], start=True, stop=True)
                    last.then_inc(LV.sem, 1)
                    pe.wait_ge(LV.sem, LV.upto(t, 4 * m + 2))
                    for hh in range(DH):
                        last = pe.matmul(bank(4)[:, hh, :], yy[:, hh, :], invT[:, hh, :], start=True, stop=True)
                    if m < LEVELS - 1:
                        for hh in range(DH):
                            last = pe.matmul(bank(3)[:, hh, :], invT[:, hh, :], yy[:, hh, :], start=True, stop=True)
                    last.then_inc(LV.sem, 1)
                return seg

            def core_b(t):
                pe.wait_ge(LV.sem, LV.upto(t, 4 * LEVELS))
                for hh in range(DH):
                    last = pe.matmul(bank(2)[:, hh, :], invT[:, hh, :], rr[:, hh, :], start=True, stop=True)
                last.then_inc(CO.sem, 1)
                pe.wait_ge(CO.sem, CO.upto(t, 8))
                for hh in range(DH):
                    pe.matmul(bank(3)[:, hh, :], intra[:, hh, :], vn[:, hh, :], start=True, stop=True)
                for hh in range(DH):
                    last = pe.matmul(bank(4)[:, hh, :], kd[:, hh, :], vn[:, hh, :], start=True, stop=True)
                last.then_inc(CO.sem, 1)

            def mix_seg(t):
                pe.wait_ge(CO.sem, CO.upto(t, 18))
                transposes(bank(0), [mix[:, P * j:P * j + P] for j in range(4)])
                transposes(bank(1), [mix[:, P * j:P * j + P] for j in range(4, 8)]).then_inc(OU.sem, 1)

            def project_out(c):
                def seg(t):
                    pe.wait_ge(OU.sem, OU.upto(t, 2))
                    if c == 0:
                        if t.first:
                            pe.wait_ge(resident_in, 16)
                        product(W[:, 2, :], hT, resident)
                    else:
                        chunk(t.tail_at, c - 1, W[:, 2 + c, :], hT)
                return seg

            def norm2_seg(t):
                pe.wait_ge(OU.sem, OU.upto(t, 7))
                transposes(bank(0), [h2[:, P * j:P * j + P] for j in range(4)])
                transposes(bank(1), [h2[:, P * j:P * j + P] for j in range(4, 8)]).then_inc(OU.sem, 1)

            def query_product(t, c):
                pe.wait_ge(OU.sem, OU.upto(t, 9))
                chunk(t.tail_at, N_OUT - 1 + c, W[:, 2 + c, :], hT)

            def query(c):
                def seg(t):
                    if t.first:
                        if c < N_QRY:
                            query_product(t, c)
                            keys(t, c)
                        return
                    if c < N_QRY:
                        query_product(t, c)
                    if c > 0:
                        keys(t, c - 1)
                return seg

            def keys(t, c):
                pe.wait_ge(QC.sem, QC.upto(t, c + 1))
                if c >= 2:
                    pe.wait_ge(QT.sem, QT.upto(t, 2 * c - 2))
                transposes(bank(c % 2), [bufA[:, CH * c + P * j:CH * c + P * j + P]
                                         for j in range(4)]).then_inc(QT.sem, 1)
                pe.wait_ge(QT.sem, QT.upto(t, 2 * c + 2))
                for j in range(4):
                    last = pe.matmul(W[:, 2 + c, P * j:P * j + P], bufB[:, CH * c + P * j:CH * c + P * j + P],
                                     keysT[:, j % 2, :], start=True, stop=True)
                last.then_inc(SC.sem, 1)

            def none(t):
                pass

            later = [level(m) for m in range(LEVELS)] + [
                core_b, mix_seg, project_out(0), project_out(1), norm2_seg] + [query(c) for c in range(N_QRY + 1)]
            tail = [transpose_seg, scores_seg, none, none, pv_seg, qk_norm_seg, decay_seg, core_a] + later + [
                none, none, none]
            segments = {
                FIRST: [norm1_seg] + [project(c) for c in range(N_IN)] + [
                    norm1_next, transpose_seg, scores_seg, project_next(0), project_next(1), pv_seg, qk_sums,
                    project_next(2), kv_transposed, decay_seg, core_a, project_next(3)]
                + later[:3] + [project_next(4)] + later[3:LEVELS + 1] + [project_next(5)] + later[LEVELS + 1:],
                BOTH: [none, norm1_seg, project(0), norm1_next, project_next(0), none]
                + [f(c) for c in range(1, N_IN) for f in (project, project_next)] + tail,
                LOADED: [none, none, none] + tail,
            }

            def slots(u, k0, k1):
                if k0 == k1:
                    return
                if k0 == 0:
                    pe.wait_ge(handed_late, u.times(1, 1))
                for k in range(k0, k1):
                    pe.wait_ge(diag_done, u.times(SLOTS, k + 1))
                    pe.wait_ge(up_in[k % RING], u.times(PER_RING, 16 * (k // RING + 1)))
                    for c in range(2):
                        last = pe.matmul(acc[:, c, :], diag[:, k % DIAGS, :],
                                         up_ring[:, k % RING, CH * c:CH * c + CH],
                                         start=k == 0, stop=k == SLOTS - 1)
                    last.then_inc(up_free, 1)

            interleaved(pe, segments, slots)

        @block.scalar
        def _(act):
            act.wait_ge(consts_in, 48)
            act.activation(gs[:, 23, :], row[:, R_AL:R_AL + DH], ACT.Exp).then_inc(negA.sem, 1)

            def norm1_seg(t):
                if not t.first:
                    act.wait_ge(idx_ready, t.number.times(1))
                act.wait_ge(x_in, t.number.times(16, 16))
                act.activation(h, xt[:, 0:D], ACT.Square, accum_out=st[:, 0:1]).then_inc(N1.sem, 1)
                act.wait_ge(N1.sem, N1.upto(t, 1))
                act.activation(st[:, 1:2], st[:, 0:1], ACT.Sqrt, bias=eps, scale=1.0 / D).then_inc(N1.sem, 1)
                act.wait_ge(N1.sem, N1.upto(t, 3))
                act.activation(h, xt[:, 0:D], ACT.Copy, scale=st[:, 2:3]).then_inc(N1.sem, 1)

            def norm1_next(t):
                nxt = NextTile(t.first)
                act.wait_ge(xb_in, t.round.times(16, 16))
                act.activation(nxt.h, nxt.x, ACT.Square, accum_out=st[:, 3:4]).then_inc(NB.sem, 1)
                act.wait_ge(NB.sem, NB.upto(t, 1))
                act.activation(st[:, 4:5], st[:, 3:4], ACT.Sqrt, bias=eps, scale=1.0 / D).then_inc(NB.sem, 1)
                act.wait_ge(NB.sem, NB.upto(t, 3))
                act.activation(nxt.h, nxt.x, ACT.Copy, scale=st[:, 5:6]).then_inc(NB.sem, 1)

            def qk_square(t):
                if t.kind == LOADED:
                    act.wait_ge(x_in, t.number.times(16, 16))
                    wait_projected(act, t)
                else:
                    act.wait_ge(in_copied, t.copied.times(1, 3 if t.kind == BOTH else 2))
                act.activation(h[:, 0:QK_W], proj[:, 0:QK_W], ACT.Square).then_inc(AT.sem, 1)

            def qk_rms(t):
                act.wait_ge(AT.sem, AT.upto(t, 2))
                act.activation(st[:, 20:30], st[:, 10:20], ACT.Sqrt, bias=eps,
                               scale=1.0 / HD).then_inc(AT.sem, 1)

            def project(c):
                def seg(t):
                    if c == 2:
                        qk_square(t)
                    if c == 3:
                        qk_rms(t)
                    n = chunk_cols(c)
                    if t.kind == BOTH:
                        act.wait_ge(FP.sem, FP.upto(t, c + 1))
                    else:
                        act.wait_ge(chunk_used, t.in_at.times(1, c + 1))
                    bank_no = 2 + (2 * c if t.kind == BOTH else c) % 4
                    act.copy(proj[:, CH * c:CH * c + n], W[:, bank_no, 0:n]).then_inc(in_copied, 1)
                return seg

            def project_next(c):
                def seg(t):
                    at = t.next_at if t.first else t.in_at
                    src = acc[:, c % 2, :] if t.first else W[:, 2 + (2 * c + 1) % 4, :]
                    act.wait_ge(chunk_used, at.times(1, c + 1))
                    act.copy(NextTile(t.first).staged(c), src[:, 0:chunk_cols(c)]).then_inc(in_copied, 1)
                return seg

            def transpose_seg(t):
                act.wait_ge(DN.sem, DN.upto(t, 2))
                for g in range(3):
                    last = act.copy(cin[:, 4 * g:4 * g + 4, CONV - 1:], bank(2 + g))
                last.then_inc(DN.sem, 1)
                act.wait_ge(AT.sem, AT.upto(t, 9))
                act.copy(qT[:, :, :], bank(0)).then_inc(AT.sem, 1)

            def scores_seg(t):
                act.wait_ge(AT.sem, AT.upto(t, 16))
                for hh in range(AH):
                    act.activation(bufA[:, 256 * hh:256 * hh + 256], bufA[:, 256 * hh:256 * hh + 256], ACT.Exp,
                                   bias=st[:, 40 + hh:41 + hh], accum_out=st[:, 56 + hh:57 + hh])
                act.activation(st[:, 64:72], st[:, 48:56], ACT.Exp).then_inc(AT.sem, 1)

            def pv_seg(t):
                act.wait_ge(PT.sem, PT.upto(t, 1))
                for b in range(2):
                    last = act.copy(bufB[:, CH * b:CH * b + CH], W[:, 2 + b, :])
                last.then_inc(PT.sem, 1)

            def qk_norm_seg(t):
                act.wait_ge(DN.sem, DN.upto(t, 9))
                act.activation(ya[:, :, :], ya[:, :, :], ACT.Silu).then_inc(DN.sem, 1)
                act.wait_ge(DN.sem, DN.upto(t, 10))
                act.activation(yb[:, 0:8, :], ya[:, 0:8, :], ACT.Square).then_inc(DN.sem, 1)
                act.wait_ge(DN.sem, DN.upto(t, 12))
                act.activation(yb[:, 0:8, :], W[:, 2:4, :].rearrange("p b (n i) -> p (b n) i", n=4), ACT.Sqrt,
                               bias=eps).then_inc(DN.sem, 1)
                act.activation(proj[:, GATE0:BETA0], proj[:, GATE0:BETA0], ACT.Silu)
                act.wait_ge(DN.sem, DN.upto(t, 16))
                act.copy(ktok, bank(4))
                act.copy(vtok, bank(5)).then_inc(SG.sem, 1)

            def gate_math(t):
                act.wait_ge(GT.sem, GT.upto(t, 3))
                act.activation(gs[:, 3, :], gs[:, 2, :], ACT.Exp)
                act.activation(gs[:, 4, :], proj[:, BETA0:BETA0 + DH], ACT.Exp, scale=-1.0).then_inc(GT.sem, 1)
                act.wait_ge(GT.sem, GT.upto(t, 6))
                act.activation(gs[:, 8, :], gs[:, 5, :], ACT.Ln).then_inc(GT.sem, 1)

            def decay_seg(t):
                act.wait_ge(GT.sem, GT.upto(t, 20))
                act.activation(dec, dec, ACT.Exp)
                act.activation(gs[:, 17:20, :], gs[:, 14:17, :], ACT.Exp).then_inc(GT.sem, 1)

            def none(t):
                pass

            def level(m):
                def seg(t):
                    act.wait_ge(LV.sem, LV.upto(t, 4 * m + 1))
                    act.copy(yy[:, :, :], bank(2)).then_inc(LV.sem, 1)
                return seg

            def core_b(t):
                act.wait_ge(CO.sem, CO.upto(t, 7))
                act.copy(vn[:, :, :], bank(2)).then_inc(CO.sem, 1)
                act.wait_ge(CO.sem, CO.upto(t, 11))
                act.activation(o_sq, o_dn, ACT.Square).then_inc(CO.sem, 1)
                act.wait_ge(CO.sem, CO.upto(t, 13))
                act.activation(gs[:, 21, :], gs[:, 20, :], ACT.Sqrt, bias=eps, scale=1.0 / DK).then_inc(CO.sem, 1)

            def mix_seg(t):
                act.wait_ge(OU.sem, OU.upto(t, 1))
                for g in range(2):
                    last = act.copy(hT[:, 4 * g:4 * g + 4, :], bank(g))
                last.then_inc(OU.sem, 1)

            def norm2_seg(t):
                act.wait_ge(OU.sem, OU.upto(t, 3))
                act.activation(h, x2[:, :], ACT.Square, accum_out=st[:, 80:81]).then_inc(OU.sem, 1)
                act.wait_ge(OU.sem, OU.upto(t, 4))
                act.activation(st[:, 81:82], st[:, 80:81], ACT.Sqrt, bias=eps, scale=1.0 / D).then_inc(OU.sem, 1)
                act.wait_ge(OU.sem, OU.upto(t, 8))
                for g in range(2):
                    last = act.copy(hT[:, 4 * g:4 * g + 4, :], bank(g))
                last.then_inc(OU.sem, 1)

            def query_out(t, c):
                act.wait_ge(chunk_used, t.tail_at.times(1, N_OUT + c))
                act.copy(bufA[:, CH * c:CH * c + CH], W[:, 2 + c, :]).then_inc(QC.sem, 1)

            def query_t_out(t, c):
                act.wait_ge(QT.sem, QT.upto(t, 2 * c + 1))
                act.copy(bufB[:, CH * c:CH * c + CH], W[:, c % 2, :]).then_inc(QT.sem, 1)

            def query(c):
                def seg(t):
                    if t.first:
                        if c < N_QRY:
                            query_out(t, c)
                            query_t_out(t, c)
                        return
                    if c < N_QRY:
                        query_out(t, c)
                    if c > 0:
                        query_t_out(t, c - 1)
                return seg

            def gate_exp(t):
                act.wait_ge(SM.sem, SM.upto(t, 1))
                act.activation(gates[:, :, :], gates[:, :, :], ACT.Exp).then_inc(SM.sem, 1)

            later = [level(m) for m in range(LEVELS)] + [
                core_b, mix_seg, none, none, norm2_seg] + [query(c) for c in range(N_QRY + 1)] + [none, gate_exp, none]
            tail = [transpose_seg, gate_math, scores_seg, none, pv_seg, qk_norm_seg, decay_seg, none] + later
            segments = {
                FIRST: [norm1_seg] + [project(c) for c in range(5)] + [
                    norm1_next, project(5), transpose_seg, gate_math, scores_seg, project_next(0), project_next(1),
                    pv_seg, qk_norm_seg, project_next(2), decay_seg, project_next(3)]
                + later[:3] + [project_next(4)] + later[3:LEVELS + 1] + [project_next(5)] + later[LEVELS + 1:],
                BOTH: [none, norm1_seg, project(0), norm1_next, project_next(0), none]
                + [f(c) for c in range(1, N_IN) for f in (project, project_next)] + tail,
                LOADED: [none, qk_square, qk_rms] + tail,
            }

            def slots(u, k0, k1):
                for k in range(k0, k1, 2):
                    act.wait_ge(down_free, u.times(SLOTS, RING + k + 2))
                    act.activation(act_s[:, k:k + 2], dots[:, k:k + 2], ACT.Gelu).then_inc(gelu_done, 1)
                    act.wait_ge(gelu_done, u.times(SLOTS // 2, k // 2 + 1))
                    for j in (k, k + 1):
                        act.activation(wgt[:, j:j + 1], act_s[:, j:j + 1], ACT.Copy,
                                       scale=gatesc[:, j:j + 1]).then_inc(wgt_done, 1)
                    act.wait_ge(wgt_done, u.times(SLOTS, k + 2))
                    for j in (k, k + 1):
                        act.wait_ge(up_free, u.times(SLOTS, j + 1))
                        act.activation(diag[:, j % DIAGS, :], ident, ACT.Copy,
                                       scale=wgt[:, j:j + 1]).then_inc(diag_done, 1)

            interleaved(act, segments, slots, DIAG_LEAD)

        @block.vector
        def _(dve):
            level_reg = dve.alloc_register("level_reg")

            def wait_before_max(stage, t, k):
                if t.number.r is None:
                    dve.wait_ge(stage.sem, stage.upto(t, k))
                    return
                dve.reg_mul(level_reg, t.number.r, t.number.mul * stage.n)
                dve.reg_add(level_reg, level_reg, t.number.add * stage.n + k)
                dve.wait_ge(consts_in, 48)
                dve.wait_ge(stage.sem, level_reg)

            dve.memset(kTw[:, :], 0.0).then_inc(cleared, 1)
            dve.memset(v2[:, :, :], 0.0).then_inc(cleared, 1)
            dve.memset(cin[:, :, :], 0.0).then_inc(cleared, 1)
            dve.memset(state[:, :, :], 0.0).then_inc(cleared, 1)
            dve.wait_ge(consts_in, 48)
            dve.wait_ge(negA.sem, 1)
            dve.tensor_scalar(gs[:, 22, :], gs[:, 23, :], -1.0, None, ALU.mult).then_inc(negA.sem, 1)
            dve.wait_ge(negA.sem, 2)
            dve.wait_ge(cleared, 4)

            def norm1_seg(t):
                dve.wait_ge(N1.sem, N1.upto(t, 2))
                dve.reciprocal(st[:, 2:3], st[:, 1:2]).then_inc(N1.sem, 1)
                dve.wait_ge(N1.sem, N1.upto(t, 5))
                for g in range(2):
                    last = dve.tensor_tensor(NextTile(t.first).own[:, 4 * g:4 * g + 4, :], bank(g),
                                             over_last(norm1[:, 4 * g:4 * g + 4], P), ALU.mult)
                last.then_inc(N1.sem, 1)

            def norm1_next(t):
                dve.wait_ge(NB.sem, NB.upto(t, 2))
                dve.reciprocal(st[:, 5:6], st[:, 4:5]).then_inc(NB.sem, 1)
                if not t.first:
                    norm1_next_t(t)

            def norm1_next_t(t):
                nxt = NextTile(t.first)
                dve.wait_ge(NB.sem, NB.upto(t, 5))
                for g in range(2):
                    last = dve.tensor_tensor(nxt.hT[:, 4 * g:4 * g + 4, :],
                                             nxt.banks[g].rearrange("p (n i) -> p n i", n=4),
                                             over_last(norm1[:, 4 * g:4 * g + 4], P), ALU.mult)
                last.then_inc(NB.sem, 1)

            def none(t):
                pass

            def qk_seg(t):
                dve.wait_ge(AT.sem, AT.upto(t, 1))
                dve.tensor_reduce(st[:, 10:20], h[:, 0:QK_W].rearrange("p (n d) -> p n d", d=HD), AX.X,
                                  ALU.add).then_inc(AT.sem, 1)
                dve.wait_ge(AT.sem, AT.upto(t, 3))
                dve.reciprocal(st[:, 30:40], st[:, 20:30]).then_inc(AT.sem, 1)
                dve.wait_ge(AT.sem, AT.upto(t, 4))
                if t.kind == BOTH:
                    dve.wait_ge(FP.sem, FP.upto(t, N_IN))
                qk3 = qk.rearrange("p (n d) -> p n d", d=HD)
                dve.tensor_tensor(qk3, proj[:, 0:QK_W].rearrange("p (n d) -> p n d", d=HD),
                                  over_last(st[:, 30:40], HD), ALU.mult).then_inc(AT.sem, 1)
                dve.wait_ge(AT.sem, AT.upto(t, 5))
                for a in range(2):
                    dve.tensor_tensor(qk2[:, 0:AH, :].rearrange("p (j a) d -> p a j d", a=2)[:, a],
                                      qk3[:, 4 * a:4 * a + 4, :],
                                      row[:, R_QK:R_QK + 256].rearrange("p (n d) -> p n d", d=HD), ALU.mult)
                dve.tensor_tensor(qk2[:, AH:, :], qk3[:, AH:, :],
                                  row[:, R_QK + 512:R_QK + QK_W].rearrange("p (n d) -> p n d", d=HD),
                                  ALU.mult).then_inc(AT.sem, 1)
                dve.wait_ge(AT.sem, AT.upto(t, 6))
                x12 = qk2[:, :, 0:ROPE].rearrange("p n (s e) -> p n s e", s=2)
                for dst, c0 in ((rope_c, D), (rope_s, D + 8)):
                    for s in range(2):
                        last = dve.tensor_tensor(dst[:, :, s, :], x12[:, :, s, :],
                                                 over_mid(xt[:, c0:c0 + 8], AH + KVH), ALU.mult)
                last.then_inc(AT.sem, 1)
                dve.wait_ge(AT.sem, AT.upto(t, 7))
                dve.tensor_tensor(x12[:, :, 0, :], rope_c[:, :, 0, :], rope_s[:, :, 1, :], ALU.subtract)
                dve.tensor_tensor(x12[:, :, 1, :], rope_c[:, :, 1, :], rope_s[:, :, 0, :],
                                  ALU.add).then_inc(AT.sem, 1)

            def transpose_seg(t):
                wait_projected(dve, t)
                dve.tensor_copy(v2[:, 0, :], v2[:, 1, :])
                dve.tensor_copy(kTw[:, 0:P], kTw[:, P:2 * P]).then_inc(MV.sem, 1)
                dve.tensor_copy(cin[:, :, 0:CONV - 1], cin[:, :, P:P + CONV - 1]).then_inc(DN.sem, 1)
                dve.wait_ge(MV.sem, MV.upto(t, 1))
                dve.tensor_copy(v2[:, 1, :], proj[:, QK_W:QK_W + P])
                dve.wait_ge(AT.sem, AT.upto(t, 9))
                dve.tensor_copy(kTw[:, P:2 * P], W[:, 1, 0:P]).then_inc(AT.sem, 1)

            def softmax_seg(t):
                c0 = C_M0 if t.first else C_M1
                if t.kind == BOTH:
                    dve.wait_ge(spilled, t.round.times(32, 32))
                s3 = bufA[:, :].rearrange("p (n k) -> p n k", n=AH)
                dve.wait_ge(AT.sem, AT.upto(t, 12))
                for b in range(4):
                    last = dve.scalar_tensor_tensor(
                        out=s3[:, 2 * b:2 * b + 2, :], in0=bank(2 + b, 2), scalar=HD ** -0.5,
                        in1=over_mid(cst[:, c0:c0 + 2 * P], 2), op0=ALU.mult, op1=ALU.add)
                last.then_inc(AT.sem, 1)
                dve.wait_ge(AT.sem, AT.upto(t, 13))
                dve.tensor_reduce(st[:, 72:80], s3, AX.X, ALU.max).then_inc(AT.sem, 1)
                dve.wait_ge(AT.sem, AT.upto(t, 14))
                dve.tensor_tensor(st[:, 72:80], st[:, 72:80], sinks, ALU.max).then_inc(AT.sem, 1)
                dve.wait_ge(AT.sem, AT.upto(t, 15))
                dve.tensor_scalar(st[:, 40:48], st[:, 72:80], -1.0, None, ALU.mult)
                dve.tensor_tensor(st[:, 48:56], sinks, st[:, 72:80], ALU.subtract).then_inc(AT.sem, 1)

            def probs_seg(t):
                dve.wait_ge(AT.sem, AT.upto(t, 17))
                dve.tensor_tensor(st[:, 84:92], st[:, 56:64], st[:, 64:72], ALU.add).then_inc(AT.sem, 1)
                dve.wait_ge(AT.sem, AT.upto(t, 18))
                dve.reciprocal(st[:, 72:80], st[:, 84:92]).then_inc(AT.sem, 1)
                dve.wait_ge(PT.sem, PT.upto(t, 1))
                for b in range(2, 4):
                    last = dve.tensor_copy(bufB[:, CH * b:CH * b + CH], W[:, 2 + b, :])
                last.then_inc(PT.sem, 1)

            def conv_seg(t):
                def tap(dst, i):
                    return dve.tensor_tensor(dst[:, :, :], cin[:, :, i:i + P], over_last(convw[:, i, :], P), ALU.mult)

                dve.wait_ge(DN.sem, DN.upto(t, 3))
                tap(ya, 0)
                tap(yb, 1).then_inc(DN.sem, 1)
                for i in range(2, CONV + 1):
                    dve.wait_ge(DN.sem, DN.upto(t, 2 * i))
                    dve.tensor_tensor(ya[:, :, :], ya[:, :, :], yb[:, :, :], ALU.add).then_inc(DN.sem, 1)
                    if i < CONV:
                        dve.wait_ge(DN.sem, DN.upto(t, 2 * i + 1))
                        tap(yb, i).then_inc(DN.sem, 1)

            def qk_norm_seg(t):
                if t.kind == LOADED:
                    dve.wait_ge(stored, t.number.before().times(16, 16))
                dve.wait_ge(AT.sem, AT.upto(t, 19))
                dve.wait_ge(PT.sem, PT.upto(t, 4))
                dve.tensor_tensor(mix[:, 0:512].rearrange("p (n d) -> p n d", d=HD), bank(0, AH),
                                  over_last(st[:, 72:80], HD), ALU.mult).then_inc(PT.sem, 1)
                dve.wait_ge(DN.sem, DN.upto(t, 13))
                dve.reciprocal(yb[:, 0:8, :], yb[:, 0:8, :]).then_inc(DN.sem, 1)
                dve.wait_ge(DN.sem, DN.upto(t, 14))
                dve.scalar_tensor_tensor(out=ya[:, 0:4, :], in0=yb[:, 0:4, :], scalar=DK ** -0.5, in1=ya[:, 0:4, :],
                                         op0=ALU.mult, op1=ALU.mult)
                dve.tensor_tensor(ya[:, 4:8, :], ya[:, 4:8, :], yb[:, 4:8, :], ALU.mult).then_inc(DN.sem, 1)

            def g(n):
                return gs[:, n, :]

            def gate_math(t):
                dve.tensor_tensor(g(0), proj[:, BETA0 + DH:IN_W], row[:, R_DT:R_DT + DH], ALU.add).then_inc(GT.sem, 1)
                dve.wait_ge(GT.sem, GT.upto(t, 1))
                dve.tensor_scalar(g(1), g(0), -1.0, None, ALU.mult).then_inc(GT.sem, 1)
                dve.wait_ge(GT.sem, GT.upto(t, 2))
                dve.tensor_tensor(g(2), g(0), g(1), ALU.min).then_inc(GT.sem, 1)
                dve.wait_ge(GT.sem, GT.upto(t, 4))
                dve.tensor_scalar(g(5), g(3), 1.0, None, ALU.add)
                dve.tensor_scalar(g(6), g(4), 1.0, None, ALU.add).then_inc(GT.sem, 1)
                dve.wait_ge(GT.sem, GT.upto(t, 5))
                dve.reciprocal(g(7), g(6)).then_inc(GT.sem, 1)
                dve.wait_ge(GT.sem, GT.upto(t, 7))
                dve.tensor_scalar(g(9), g(5), -1.0, None, ALU.add)
                dve.tensor_scalar(g(10), g(5), 1.0, None, ALU.is_equal).then_inc(GT.sem, 1)
                dve.wait_ge(GT.sem, GT.upto(t, 8))
                dve.tensor_tensor(g(9), g(9), g(10), ALU.add)
                dve.tensor_tensor(g(8), g(8), g(10), ALU.add).then_inc(GT.sem, 1)
                dve.wait_ge(GT.sem, GT.upto(t, 9))
                dve.reciprocal(g(11), g(9))
                dve.tensor_tensor(g(12), g(8), g(3), ALU.mult).then_inc(GT.sem, 1)
                dve.wait_ge(GT.sem, GT.upto(t, 10))
                dve.tensor_tensor(g(12), g(12), g(11), ALU.mult).then_inc(GT.sem, 1)
                dve.tensor_scalar(g(1), g(0), 0.0, None, ALU.max).then_inc(GT.sem, 1)
                dve.wait_ge(GT.sem, GT.upto(t, 12))
                dve.tensor_tensor(g(12), g(12), g(1), ALU.add).then_inc(GT.sem, 1)
                dve.wait_ge(GT.sem, GT.upto(t, 13))
                dve.tensor_tensor(g(13), g(12), g(22), ALU.mult).then_inc(GT.sem, 1)

            def decay_seg(t):
                dve.wait_ge(GT.sem, GT.upto(t, 15))
                dve.tensor_copy(g(16), W[:, 0, 0:DH]).then_inc(GT.sem, 1)
                dve.wait_ge(GT.sem, GT.upto(t, 16))
                dve.tensor_tensor(dg, over_mid(ident, DH), over_last(g(16), P), ALU.mult)
                dve.tensor_tensor(db, over_mid(ident, DH), over_last(g(7), P), ALU.mult).then_inc(GT.sem, 1)
                dve.wait_ge(GT.sem, GT.upto(t, 18))
                for hh in range(DH):
                    dve.tensor_scalar(dec[:, hh, :], bank(0)[:, hh, :], gs[:, 16, hh:hh + 1], 0.0,
                                      ALU.subtract, ALU.min)
                dve.tensor_tensor(g(14), bank(0)[:, :, P - 1], g(16), ALU.subtract)
                dve.tensor_copy(g(15), bank(0)[:, :, P - 1]).then_inc(GT.sem, 1)
                dve.wait_ge(GT.sem, GT.upto(t, 19))
                dve.tensor_scalar(g(14), g(14), 0.0, None, ALU.min).then_inc(GT.sem, 1)
                dve.wait_ge(GT.sem, GT.upto(t, 21))
                dve.tensor_tensor(dec, dec, over_mid(tri, DH), ALU.mult)
                dve.tensor_tensor(gs[:, 20, :], g(7), g(19), ALU.mult)

            def masked(t, m):
                return dve.tensor_tensor(lm[:, m % 2], lt, over_mid(levels[:, m, :], DH), ALU.mult)

            def core_a(t):
                dve.wait_ge(CO.sem, CO.upto(t, 2))
                dve.tensor_copy(inv, over_mid(ident, DH))
                dve.tensor_copy(invT, over_mid(ident, DH)).then_inc(CO.sem, 1)
                dve.wait_ge(CO.sem, CO.upto(t, 3))
                dve.tensor_tensor(lt, bank(2), dec, ALU.mult).then_inc(CO.sem, 1)
                dve.tensor_tensor(intra, bank(3), dec, ALU.mult)
                dve.wait_ge(CO.sem, CO.upto(t, 4))
                dve.tensor_tensor(lt, lt, bank(1), ALU.mult).then_inc(CO.sem, 1)
                dve.wait_ge(SG.sem, SG.upto(t, 1))
                dve.tensor_tensor(ks_s, bank(5), over_last(gs[:, 20, :], P), ALU.mult)
                dve.tensor_tensor(vb, vtok, over_last(gs[:, 7, :], P), ALU.mult)
                dve.tensor_tensor(qs_s, bank(0), over_last(gs[:, 19, :], P), ALU.mult)
                dve.wait_ge(CO.sem, CO.upto(t, 5))
                masked(t, 0).then_inc(LM.sem, 1)
                dve.wait_ge(LM.sem, LM.upto(t, 1))
                dve.tensor_tensor(rr, vb, ks_s, ALU.subtract).then_inc(CO.sem, 1)
                dve.tensor_tensor(kd, ktok, over_last(gs[:, 17, :], P), ALU.mult)

            def level(m):
                def seg(t):
                    if m < LEVELS - 1:
                        masked(t, m + 1).then_inc(LM.sem, 1)
                    dve.wait_ge(LV.sem, LV.upto(t, 4 * m + 3))
                    if m < LEVELS - 1:
                        dve.tensor_tensor(inv, inv, bank(3), ALU.subtract)
                    dve.tensor_tensor(invT, invT, bank(4), ALU.subtract).then_inc(LV.sem, 1)
                return seg

            def core_b(t):
                dve.wait_ge(CO.sem, CO.upto(t, 9))
                dve.tensor_tensor(o_dn, qs_s, bank(3), ALU.add)
                dve.tensor_tensor(state[:, :, :], state[:, :, :], over_last(gs[:, 18, :], P),
                                  ALU.mult).then_inc(CO.sem, 1)
                dve.wait_ge(CO.sem, CO.upto(t, 10))
                dve.tensor_tensor(state[:, :, :], state[:, :, :], bank(4), ALU.add).then_inc(CO.sem, 1)
                dve.wait_ge(CO.sem, CO.upto(t, 12))
                dve.tensor_reduce(gs[:, 20, :], o_sq, AX.X, ALU.add).then_inc(CO.sem, 1)
                dve.wait_ge(CO.sem, CO.upto(t, 14))
                dve.reciprocal(gs[:, 20, :], gs[:, 21, :]).then_inc(CO.sem, 1)
                dve.wait_ge(CO.sem, CO.upto(t, 15))
                dve.tensor_tensor(o_dn, o_dn, over_last(gs[:, 20, :], P), ALU.mult).then_inc(CO.sem, 1)
                dve.wait_ge(CO.sem, CO.upto(t, 16))
                dve.tensor_tensor(o_dn, o_dn, over_mid(dn_w, DH), ALU.mult).then_inc(CO.sem, 1)
                dve.wait_ge(CO.sem, CO.upto(t, 17))
                dve.tensor_tensor(mix[:, 512:D], flat(o_dn), proj[:, GATE0:BETA0], ALU.mult).then_inc(CO.sem, 1)

            def out_seg(t):
                dve.wait_ge(chunk_used, t.tail_at.times(1, N_OUT - 1))
                dve.tensor_tensor(x2[:, :], xt[:, 0:D], flat(W[:, 2:4, :]), ALU.add).then_inc(OU.sem, 1)

            def norm2_seg(t):
                dve.wait_ge(OU.sem, OU.upto(t, 5))
                dve.reciprocal(st[:, 82:83], st[:, 81:82]).then_inc(OU.sem, 1)
                dve.wait_ge(OU.sem, OU.upto(t, 6))
                dve.scalar_tensor_tensor(out=h2[:, :], in0=x2[:, :], scalar=st[:, 82:83], in1=norm2,
                                         op0=ALU.mult, op1=ALU.mult).then_inc(OU.sem, 1)

            s_in = flat(W[:, 2:6, :]).rearrange("p (n k) -> p n k", k=NKEY)

            def top(c):
                items, heads = range(4 * c, 4 * c + 4), range(2 * c, 2 * c + 2)
                sc2 = proj[:, 0:512].rearrange("p (n k) -> p n k", n=4)
                left = proj[:, 512:1024].rearrange("p (n k) -> p n k", n=2)
                own = proj[:, 1024:2048].rearrange("p (s m k) -> p s m k", s=2, k=TOPK)
                cand = bufA[:, CH * c:CH * c + CH].rearrange("p (n a b) -> p n a b", a=TOPK, b=TOPK)
                sums = bufA[:, CH * c:CH * c + CH].rearrange("p (n k) -> p n k", n=2)
                mine = slice(2 * TOPK * c, 2 * TOPK * c + 2 * TOPK)
                v_h = v16[:, 4 * c:4 * c + 4, :].rearrange("p (n s) k -> p n s k", s=2)
                i_h = i16f[:, 4 * c:4 * c + 4, :].rearrange("p (n s) k -> p n s k", s=2)

                def seg(t):
                    def after(k):
                        wait_before_max(TK, t, 15 * c + k)

                    wait_before_max(SC, t, c + 1)
                    for n in items:
                        last = dve.max(v16[:, n, 0:8], s_in[:, n, :])
                    last.then_inc(TK.sem, 1)
                    after(1)
                    for j, n in enumerate(items):
                        last = dve.match_replace(sc2[:, j, :], v16[:, n, 0:8], s_in[:, n, :], -3e38)
                    last.then_inc(TK.sem, 1)
                    after(2)
                    for j, n in enumerate(items):
                        last = dve.max(v16[:, n, 8:16], sc2[:, j, :])
                    last.then_inc(TK.sem, 1)
                    for n in items:
                        dve.max_index(i16[:, n, 0:8], v16[:, n, 0:8], s_in[:, n, :])
                    after(3)
                    for j, n in enumerate(items):
                        last = dve.max_index(i16[:, n, 8:16], v16[:, n, 8:16], sc2[:, j, :])
                    last.then_inc(TK.sem, 1)
                    for j in range(2):
                        last = dve.tensor_tensor(cand[:, j], over_last(v_h[:, j, 0, :], TOPK),
                                                 over_mid(v_h[:, j, 1, :], TOPK), ALU.add)
                    last.then_inc(TK.sem, 1)
                    after(5)
                    for j, n in enumerate(heads):
                        last = dve.max(top_s[:, n, 0:8], sums[:, j, :])
                    last.then_inc(TK.sem, 1)
                    after(6)
                    for j, n in enumerate(heads):
                        last = dve.match_replace(left[:, j, :], top_s[:, n, 0:8], sums[:, j, :], -3e38)
                    last.then_inc(TK.sem, 1)
                    after(7)
                    for j, n in enumerate(heads):
                        last = dve.max(top_s[:, n, 8:16], left[:, j, :])
                    last.then_inc(TK.sem, 1)
                    for j, n in enumerate(heads):
                        dve.max_index(sel[:, n, 0:8], top_s[:, n, 0:8], sums[:, j, :])
                    after(8)
                    for j, n in enumerate(heads):
                        last = dve.max_index(sel[:, n, 8:16], top_s[:, n, 8:16], left[:, j, :])
                    last.then_inc(TK.sem, 1)
                    dve.wait_ge(TK.sem, TK.upto(t, 15 * c + 9))
                    dve.tensor_scalar(sab[:, 0, mine], flat(sel[:, 2 * c:2 * c + 2, :]), 4, None,
                                      ALU.logical_shift_right)
                    dve.tensor_scalar(sab[:, 1, mine], flat(sel[:, 2 * c:2 * c + 2, :]), TOPK - 1, None,
                                      ALU.bitwise_and).then_inc(TK.sem, 1)
                    dve.wait_ge(TK.sem, TK.upto(t, 15 * c + 10))
                    dve.tensor_copy(sabf[:, :, mine], sab[:, :, mine])
                    dve.tensor_copy(i16f[:, 4 * c:4 * c + 4, :], i16[:, 4 * c:4 * c + 4, :]).then_inc(TK.sem, 1)
                    dve.wait_ge(TK.sem, TK.upto(t, 15 * c + 11))
                    for s_ in range(2):
                        last = dve.tensor_tensor(own[:, s_], over_last(sabf[:, s_, mine], TOPK),
                                                 over_mid(iota16, 2 * TOPK), ALU.is_equal)
                    last.then_inc(TK.sem, 1)
                    dve.wait_ge(TK.sem, TK.upto(t, 15 * c + 12))
                    for s_ in range(2):
                        for j in range(2):
                            part = own[:, s_, TOPK * j:TOPK * j + TOPK, :]
                            last = dve.tensor_tensor(part, part, over_mid(i_h[:, j, s_, :], TOPK), ALU.mult)
                    last.then_inc(TK.sem, 1)
                    dve.wait_ge(TK.sem, TK.upto(t, 15 * c + 13))
                    for s_ in range(2):
                        last = dve.tensor_reduce(pick[:, s_, mine], own[:, s_], AX.X, ALU.add)
                    last.then_inc(TK.sem, 1)
                    dve.wait_ge(TK.sem, TK.upto(t, 15 * c + 14))
                    dve.scalar_tensor_tensor(out=idx[:, mine], in0=pick[:, 0, mine], scalar=float(NKEY),
                                             in1=pick[:, 1, mine], op0=ALU.mult, op1=ALU.add).then_inc(TK.sem, 1)
                    if t.first and c == 0:
                        dve.wait_ge(TK.sem, 15)
                        dve.tensor_copy(idxc[:, mine], idx[:, mine])
                        dve.tensor_copy(idxu[:, mine], idx[:, mine]).then_inc(idx_first, 1)
                return seg

            def gate_seg(t):
                dve.tensor_tensor(gates[:, :, :], top_s[:, :, :], over_last(top_s[:, :, 0], TOPK),
                                  ALU.subtract).then_inc(SM.sem, 1)
                dve.wait_ge(SM.sem, SM.upto(t, 2))
                dve.tensor_reduce(gsum[:, 0, :], gates[:, :, :], AX.X, ALU.add).then_inc(SM.sem, 1)
                dve.wait_ge(SM.sem, SM.upto(t, 3))
                dve.reciprocal(gsum[:, 1, :], gsum[:, 0, :]).then_inc(SM.sem, 1)
                dve.wait_ge(SM.sem, SM.upto(t, 4))
                dve.tensor_tensor(gates[:, :, :], gates[:, :, :], over_last(gsum[:, 1, :], TOPK),
                                  ALU.mult).then_inc(idx_ready, 1)

            tail = [transpose_seg, gate_math, softmax_seg, conv_seg, probs_seg, qk_norm_seg, decay_seg, core_a] + [
                level(m) for m in range(LEVELS)] + [core_b, none, none, out_seg, norm2_seg] + [
                none, none] + [top(c) for c in range(N_QRY)] + [gate_seg, none]
            segments = {
                FIRST: [norm1_seg, qk_seg, norm1_next, transpose_seg, norm1_next_t] + tail[1:],
                BOTH: [none, norm1_seg, none, norm1_next, none, none] + [none] * 9 + [qk_seg] + tail,
                LOADED: [none, none, qk_seg] + tail,
            }

            def slots(u, k0, k1):
                for k in range(k0, k1):
                    dve.wait_ge(down_in[k % RING], u.times(PER_RING, 16 * (k // RING + 1)))
                    down = down_ring[:, k % RING, :]
                    dve.tensor_tensor_reduce(out=down, in0=down, in1=h2c[:, :], scale=1.0, scalar=0.0,
                                             op0=ALU.mult, op1=ALU.add, accum_out=dots[:, k:k + 1]).then_inc(down_free, 1)

            def hand(t):
                if not is_first(t):
                    dve.wait_ge(down_free, t.times(SLOTS, RING))
                    dve.wait_ge(wgt_done, t.times(SLOTS))
                dve.wait_ge(idx_ready, t.times(1, 1))
                k0 = 2 * TOPK if is_first(t) else 0
                dve.tensor_copy(idxc[:, k0:], idx[:, k0:])
                dve.tensor_copy(idxu[:, k0:HALF], idx[:, k0:HALF])
                dve.tensor_copy(gatesc[:, :], flat(gates[:, :, :]))
                dve.tensor_copy(h2c[:, :], h2[:, :]).then_inc(handed, 1)
                dve.wait_ge(handed, t.times(1, 1))

            def final(u, t):
                if u is not None:
                    dve.wait_ge(up_free, u.times(SLOTS, DIAGS + SLOTS))
                    if t is None:
                        dve.wait_ge(stored, u.times(16, 16))
                    dve.tensor_tensor(out_sb[:, :], x2c[:, :], flat(acc[:, :, :]), ALU.add).then_inc(out_ready, 1)
                    dve.wait_ge(out_ready, u.times(1, 1))
                if t is not None:
                    dve.tensor_copy(idxu[:, HALF:SLOTS], idx[:, HALF:SLOTS])
                    dve.tensor_copy(x2c[:, :], x2[:, :]).then_inc(handed_late, 1)

            dve.sem_inc(down_free, RING)
            interleaved(dve, segments, slots, DOT_LEAD, hand, final)


def kernel(x, norm1_w, w_in, att_q_norm, att_k_norm, att_sinks, dn_conv_w, dn_A_log, dn_dt_bias, dn_out_norm,
           w_out, norm2_w, peer_w_query, peer_sub_keys1, peer_sub_keys2, peer_expert_down, peer_expert_up):
    import concourse.bacc as bacc
    from concourse.bass_utils import run_bass_kernel_spmd

    inv_freq = np.float32(500000.0) ** (-(np.arange(8, dtype=np.float32) * np.float32(2.0) / np.float32(ROPE)))
    ang = np.arange(SEQ, dtype=np.float32)[:, None] * inv_freq[None, :].astype(np.float32)
    i = np.arange(P)
    masks = [((i[None, :] // (2 * s) == i[:, None] // (2 * s)) & ((i[None, :] // s) % 2 == 1)
              & ((i[:, None] // s) % 2 == 0)) for s in (1 << m for m in range(LEVELS))]
    key = np.arange(2 * P)[None, :]
    valid = (key > i[:, None]) & (key <= i[:, None] + P)
    consts = np.concatenate(
        [np.eye(P), np.ones((P, P)), i[None, :] >= i[:, None]] + masks
        + [np.where(valid & (key >= P), 0.0, NEG), np.where(valid, 0.0, NEG),
           np.tile(np.arange(TOPK), (P, 1)), np.full((P, 1), EPS)], axis=1).astype(np.float32)

    def chunks(w):
        out_ = np.zeros((-(-w.shape[1] // CH), P, KT * CH), np.float32)
        for c in range(out_.shape[0]):
            part = w[:, c * CH:(c + 1) * CH]
            n = part.shape[1]
            out_[c, :, :KT * n] = part.reshape(KT, P, n).transpose(1, 0, 2).reshape(P, KT * n)
        return out_

    arrays = {
        "x_rope": np.concatenate([x[0], np.cos(ang), np.sin(ang)], axis=1),
        "weights": np.concatenate([chunks(w_in[0]), chunks(w_out[0]), chunks(peer_w_query[0])]),
        "experts_down": peer_expert_down[0],
        "experts_up": peer_expert_up[0],
        "rows": np.concatenate([np.tile(att_q_norm[0], AH), np.tile(att_k_norm[0], KVH), dn_dt_bias[0], dn_A_log[0],
                                att_sinks[0], dn_out_norm[0], norm2_w[0]])[None, :],
        "cols": np.concatenate([norm1_w[0].reshape(KT, P).T,
                                dn_conv_w[0].reshape(CONV, 12, P).transpose(2, 0, 1).reshape(P, CONV * 12),
                                peer_sub_keys1[0].T, peer_sub_keys2[0].T], axis=1),
        "consts": consts,
    }
    nc = bacc.Bacc("TRN2", target_bir_lowering=False, num_devices=1)
    arrays = {n: np.ascontiguousarray(a) for n, a in arrays.items()}
    aps = [nc.dram_tensor(n, a.shape, mybir.dt.from_np(a.dtype), kind="ExternalInput").ap()
           for n, a in arrays.items()]
    out = nc.dram_tensor("out", (SEQ, D), F32, kind="ExternalOutput").ap()
    spill = nc.dram_tensor("spill", (P, IN_W), F32, kind="Internal").ap()
    build(nc, *aps, spill, out)
    r = run_bass_kernel_spmd(nc, [arrays], core_ids=[0])
    return r.results[0]["out"].reshape(1, SEQ, D)
```
